# Optimizing a Trainium2 kernel written in Bass

```python
import jax, jax.numpy as jnp
from jax import lax
import numpy as np

D_MODEL = 1024
BATCH = 1
SEQ = 256
DEPTH = 2
DEC_BATCH = 8
DEC_SEQ = 8
PAST_LEN = 256
PAGE_SIZE = 128

N_A_LAYERS = DEPTH // 2
N_B_LAYERS = DEPTH - N_A_LAYERS
A_HEADS = 8
A_DV = D_MODEL // A_HEADS
A_DK = A_DV // 2
A_HK = A_HEADS * A_DK
A_HV = A_HEADS * A_DV
A_PROJ = 2 * A_HK + 2 * A_HV + 2 * A_HEADS
MLSTM_CHUNK = 64
B_HEADS = 8
B_HD = D_MODEL // B_HEADS
B_HW = B_HEADS * B_HD
MOBA_BLOCK = 256
MOBA_TOPK = 3
PROMPT_Q_BLOCK = 16
D_FF = 2816
EPS = 1e-6

kernel_name = "yoco_mlstm_moba_macaron_step"

F32 = jnp.float32

def rmsnorm(x, g):
    xf = x.astype(F32)
    y = xf * lax.rsqrt(jnp.mean(xf * xf, axis=-1, keepdims=True) + EPS)
    return (y * g.astype(F32)).astype(x.dtype)

def swiglu(h, w_in, w_out):
    gu = h @ w_in
    g, u = jnp.split(gu, 2, axis=-1)
    return (jax.nn.silu(g) * u) @ w_out

def alibi_slopes():
    return 2.0 ** (-8.0 * jnp.arange(1, B_HEADS + 1, dtype=F32) / B_HEADS)

def mlstm_cell(q, k, v, logi, logf, c0, n0, m0, chunk):
    bt, t, nh, _ = q.shape
    dv = v.shape[-1]
    nc = t // chunk

    def to_chunks(a):
        return a.astype(F32).reshape(bt, nc, chunk, nh, -1).transpose(1, 0, 3, 2, 4)

    def gate_chunks(a):
        return a.astype(F32).reshape(bt, nc, chunk, nh).transpose(1, 0, 3, 2)

    causal = jnp.tril(jnp.ones((chunk, chunk), dtype=bool))

    def step(carry, inp):
        c, n, m = carry
        qc, kc, vc, li, lf = inp
        b = jnp.cumsum(lf, axis=-1)
        d = jnp.where(causal, b[..., :, None] - b[..., None, :] + li[..., None, :], -jnp.inf)
        inter = b + m[..., None]
        m_loc = jnp.maximum(inter, jnp.max(d, axis=-1))
        w_intra = jnp.exp(d - m_loc[..., None])
        w_inter = jnp.exp(inter - m_loc)
        sw = jnp.einsum('bhtd,bhsd->bhts', qc, kc) * w_intra
        num = w_inter[..., None] * jnp.einsum('bhtd,bhde->bhte', qc, c) + jnp.einsum('bhts,bhse->bhte', sw, vc)
        qn = w_inter * jnp.einsum('bhtd,bhd->bht', qc, n) + jnp.sum(sw, axis=-1)
        den = jnp.maximum(jnp.abs(qn), jnp.exp(-m_loc))
        hc = num / den[..., None]
        b_last = b[..., -1]
        g = b_last[..., None] - b + li
        m_new = jnp.maximum(b_last + m, jnp.max(g, axis=-1))
        a = jnp.exp(b_last + m - m_new)
        w = jnp.exp(g - m_new[..., None])
        c_new = a[..., None, None] * c + jnp.einsum('bhs,bhsd,bhse->bhde', w, kc, vc)
        n_new = a[..., None] * n + jnp.einsum('bhs,bhsd->bhd', w, kc)
        return (c_new, n_new, m_new), hc

    xs = (to_chunks(q), to_chunks(k), to_chunks(v), gate_chunks(logi), gate_chunks(logf))
    (c, n, m), hs = lax.scan(step, (c0.astype(F32), n0.astype(F32), m0.astype(F32)), xs)
    h = hs.transpose(1, 0, 3, 2, 4).reshape(bt, t, nh, dv)
    return h, c, n, m

def mlstm_mixer(h, w_in, b_gate, g_head, w_out, c0, n0, m0, chunk):
    bt, t, _ = h.shape
    proj = h @ w_in
    q, k, v, o, gates = jnp.split(proj, [A_HK, 2 * A_HK, 2 * A_HK + A_HV, 2 * A_HK + 2 * A_HV], axis=-1)
    q = q.reshape(bt, t, A_HEADS, A_DK)
    k = k.reshape(bt, t, A_HEADS, A_DK) * (A_DK ** -0.5)
    v = v.reshape(bt, t, A_HEADS, A_DV)
    gates = gates.astype(F32) + b_gate.astype(F32)
    logi = gates[..., :A_HEADS]
    logf = jax.nn.log_sigmoid(gates[..., A_HEADS:])
    hc, c, n, m = mlstm_cell(q, k, v, logi, logf, c0, n0, m0, chunk)
    hn = hc * lax.rsqrt(jnp.mean(hc * hc, axis=-1, keepdims=True) + EPS)
    hn = hn.reshape(bt, t, A_HV) * g_head.astype(F32)
    out = (jax.nn.sigmoid(o.astype(F32)) * hn).astype(h.dtype) @ w_out
    return out, c, n, m

def moba_attention(q, k, v, q_pos, q_block):
    bt, tq, nh, hd = q.shape
    tk = k.shape[1]
    nb = -(-tk // MOBA_BLOCK)
    pad = nb * MOBA_BLOCK - tk
    kb = jnp.pad(k, ((0, 0), (0, pad), (0, 0), (0, 0))).reshape(bt, nb, MOBA_BLOCK, nh, hd)
    vb = jnp.pad(v, ((0, 0), (0, pad), (0, 0), (0, 0))).reshape(bt, nb, MOBA_BLOCK, nh, hd)
    k_mean = jnp.mean(kb.astype(F32), axis=2)
    n_sel = min(MOBA_TOPK, nb)
    slopes = alibi_slopes()
    scale = hd ** -0.5
    b_idx = jnp.arange(bt)[:, None, None, None]
    h_idx = jnp.arange(nh)[None, None, :, None]
    blk_off = jnp.arange(MOBA_BLOCK, dtype=jnp.int32)
    nq = tq // q_block
    qs = q.reshape(bt, nq, q_block, nh, hd).transpose(1, 0, 2, 3, 4)
    ps = q_pos.reshape(nq, q_block)

    def attend(args):
        qc, pc = args
        own = pc // MOBA_BLOCK
        qf = qc.astype(F32)
        gate = jnp.einsum('bqhd,bnhd->bqhn', qf, k_mean)
        past = jnp.arange(nb)[None, :] < own[:, None]
        gate = jnp.where(past[None, :, None, :], gate, -jnp.inf)
        top_val, top_idx = lax.top_k(gate, n_sel)
        own_b = jnp.broadcast_to(own[None, :, None, None], (bt, q_block, nh, 1)).astype(top_idx.dtype)
        idx = jnp.concatenate([top_idx, own_b], axis=-1)
        ok = jnp.concatenate([jnp.isfinite(top_val), jnp.ones((bt, q_block, nh, 1), dtype=bool)], axis=-1)
        kg = kb[b_idx, idx, :, h_idx]
        vg = vb[b_idx, idx, :, h_idx]
        key_pos = idx[..., None] * MOBA_BLOCK + blk_off
        dist = pc[None, :, None, None, None] - key_pos
        s = jnp.einsum('bqhd,bqhnkd->bqhnk', qf, kg.astype(F32)) * scale
        s = s - slopes[None, None, :, None, None] * dist.astype(F32)
        s = jnp.where(ok[..., None] & (dist >= 0), s, -jnp.inf)
        p = jax.nn.softmax(s.reshape(bt, q_block, nh, -1), axis=-1).reshape(s.shape)
        out = jnp.einsum('bqhnk,bqhnkd->bqhd', p, vg.astype(F32))
        return out.astype(q.dtype)

    out = lax.map(attend, (qs, ps))
    return out.transpose(1, 0, 2, 3, 4).reshape(bt, tq, nh, hd)

def trunk(x, c_in, n_in, m_in, k_past, v_past, q_pos, chunk, q_block,
          g_norm, w_ffn_in, w_ffn_out, w_in_a, b_gate_a, g_head_a, w_out_a,
          g_kv, w_kv, w_q_b, w_out_b, g_final):
    bt, t, _ = x.shape
    cs, ns, ms = [], [], []
    k_new = v_new = k_all = v_all = None
    for l in range(DEPTH):
        x = x + 0.5 * swiglu(rmsnorm(x, g_norm[l, 0]), w_ffn_in[l, 0], w_ffn_out[l, 0])
        h = rmsnorm(x, g_norm[l, 1])
        if l < N_A_LAYERS:
            out, c, n, m = mlstm_mixer(h, w_in_a[l], b_gate_a[l], g_head_a[l], w_out_a[l],
                                       c_in[l], n_in[l], m_in[l], chunk)
            cs.append(c); ns.append(n); ms.append(m)
        else:
            j = l - N_A_LAYERS
            q = (h @ w_q_b[j]).reshape(bt, t, B_HEADS, B_HD)
            att = moba_attention(q, k_all, v_all, q_pos, q_block)
            out = att.reshape(bt, t, B_HW) @ w_out_b[j]
        x = x + out
        x = x + 0.5 * swiglu(rmsnorm(x, g_norm[l, 2]), w_ffn_in[l, 1], w_ffn_out[l, 1])
        if l == N_A_LAYERS - 1:
            kv = rmsnorm(x, g_kv) @ w_kv
            k_new, v_new = jnp.split(kv, 2, axis=-1)
            k_new = k_new.reshape(bt, t, B_HEADS, B_HD)
            v_new = v_new.reshape(bt, t, B_HEADS, B_HD)
            if k_past is None:
                k_all, v_all = k_new, v_new
            else:
                k_all = jnp.concatenate([k_past.astype(k_new.dtype), k_new], axis=1)
                v_all = jnp.concatenate([v_past.astype(v_new.dtype), v_new], axis=1)
    y = rmsnorm(x, g_final)
    return y, jnp.stack(cs), jnp.stack(ns), jnp.stack(ms), k_new, v_new

def setup_inputs(seed: int = 0) -> dict:
    key = jax.random.key(seed)
    ks = jax.random.split(key, 24)
    n_pages = PAST_LEN // PAGE_SIZE
    n_pool = (DEC_BATCH * n_pages * 5) // 4
    nrm = jax.random.normal
    x_prompt = nrm(ks[0], (BATCH, SEQ, D_MODEL), F32)
    x_sample = nrm(ks[1], (DEC_BATCH, DEC_SEQ, D_MODEL), F32)
    state_c = 0.1 * nrm(ks[2], (N_A_LAYERS, DEC_BATCH, A_HEADS, A_DK, A_DV), F32)
    state_n = 0.1 * nrm(ks[3], (N_A_LAYERS, DEC_BATCH, A_HEADS, A_DK), F32)
    state_m = 0.5 * nrm(ks[4], (N_A_LAYERS, DEC_BATCH, A_HEADS), F32)
    cache_k = nrm(ks[5], (n_pool, PAGE_SIZE, B_HEADS, B_HD), F32)
    cache_v = nrm(ks[6], (n_pool, PAGE_SIZE, B_HEADS, B_HD), F32)
    page_table = jax.random.permutation(ks[7], n_pool)[:DEC_BATCH * n_pages].reshape(DEC_BATCH, n_pages).astype(jnp.int32)
    g_norm = 1.0 + 0.02 * nrm(ks[8], (DEPTH, 3, D_MODEL), F32)
    w_ffn_in = nrm(ks[9], (DEPTH, 2, D_MODEL, 2 * D_FF), F32) * D_MODEL ** -0.5
    w_ffn_out = nrm(ks[10], (DEPTH, 2, D_FF, D_MODEL), F32) * D_FF ** -0.5
    w_in_a = nrm(ks[11], (N_A_LAYERS, D_MODEL, A_PROJ), F32) * D_MODEL ** -0.5
    b_gate_a = jnp.concatenate([0.1 * nrm(ks[12], (N_A_LAYERS, A_HEADS), F32),
                                3.0 + 0.1 * nrm(ks[13], (N_A_LAYERS, A_HEADS), F32)], axis=-1)
    g_head_a = 1.0 + 0.02 * nrm(ks[14], (N_A_LAYERS, A_HV), F32)
    w_out_a = nrm(ks[15], (N_A_LAYERS, A_HV, D_MODEL), F32) * A_HV ** -0.5
    g_kv = 1.0 + 0.02 * nrm(ks[16], (D_MODEL,), F32)
    w_kv = nrm(ks[17], (D_MODEL, 2 * B_HW), F32) * D_MODEL ** -0.5
    w_q_b = nrm(ks[18], (N_B_LAYERS, D_MODEL, B_HW), F32) * D_MODEL ** -0.5
    w_out_b = nrm(ks[19], (N_B_LAYERS, B_HW, D_MODEL), F32) * B_HW ** -0.5
    g_final = 1.0 + 0.02 * nrm(ks[20], (D_MODEL,), F32)
    return {"x_prompt": x_prompt, "x_sample": x_sample, "state_c": state_c, "state_n": state_n,
            "state_m": state_m, "cache_k": cache_k, "cache_v": cache_v, "page_table": page_table,
            "g_norm": g_norm, "w_ffn_in": w_ffn_in, "w_ffn_out": w_ffn_out, "w_in_a": w_in_a,
            "b_gate_a": b_gate_a, "g_head_a": g_head_a, "w_out_a": w_out_a, "g_kv": g_kv,
            "w_kv": w_kv, "w_q_b": w_q_b, "w_out_b": w_out_b, "g_final": g_final}

def reference(x_prompt, x_sample, state_c, state_n, state_m, cache_k, cache_v, page_table,
              g_norm, w_ffn_in, w_ffn_out, w_in_a, b_gate_a, g_head_a, w_out_a,
              g_kv, w_kv, w_q_b, w_out_b, g_final):
    weights = (g_norm, w_ffn_in, w_ffn_out, w_in_a, b_gate_a, g_head_a, w_out_a,
               g_kv, w_kv, w_q_b, w_out_b, g_final)
    bp, tp, _ = x_prompt.shape
    bs, ts, _ = x_sample.shape
    c0 = jnp.zeros((N_A_LAYERS, bp, A_HEADS, A_DK, A_DV), F32)
    n0 = jnp.zeros((N_A_LAYERS, bp, A_HEADS, A_DK), F32)
    m0 = jnp.zeros((N_A_LAYERS, bp, A_HEADS), F32)
    pos_p = jnp.arange(tp, dtype=jnp.int32)
    y_prompt, c_prompt, n_prompt, m_prompt, k_prompt, v_prompt = trunk(
        x_prompt, c0, n0, m0, None, None, pos_p, min(MLSTM_CHUNK, tp), PROMPT_Q_BLOCK, *weights)
    past_len = page_table.shape[1] * cache_k.shape[1]
    k_past = cache_k[page_table].reshape(bs, past_len, B_HEADS, B_HD)
    v_past = cache_v[page_table].reshape(bs, past_len, B_HEADS, B_HD)
    pos_s = past_len + jnp.arange(ts, dtype=jnp.int32)
    y_sample, c_sample, n_sample, m_sample, k_sample, v_sample = trunk(
        x_sample, state_c, state_n, state_m, k_past, v_past, pos_s, ts, 1, *weights)
    return (y_prompt, y_sample, c_prompt, n_prompt, m_prompt, k_prompt, v_prompt,
            c_sample, n_sample, m_sample, k_sample, v_sample)


_drawn_inputs = setup_inputs


def setup_inputs(seed=0):
    import zlib

    import numpy as np

    out = dict(_drawn_inputs(seed))
    spreads = {}
    factors = {'g_head_a': 5.491, 'g_kv': 8.074, 'g_final': 8.649}
    for name, (base, spread) in spreads.items():
        noise = np.random.default_rng([zlib.crc32(name.encode()), seed]).standard_normal(out[name].shape)
        drawn = base * np.exp(spread * noise) if base else spread * noise
        out[name] = __import__('jax').numpy.asarray(drawn.astype(out[name].dtype))
    for name, factor in factors.items():
        out[name] = (out[name] * factor).astype(out[name].dtype)
    return out
```

```python
from contextlib import ExitStack

import concourse.bass as bass
from concourse import mybir

D = 1024
KT = D // 128
TP, NB, TS = 256, 8, 8
NS = NB * TS
T = TP + NS
FF = 2816
FK = FF // 128
HALF = FK // 2
H = 8
DK, DV = 64, 128
HP = H // 2
PAST, PAGE = 256, 128
NPG = PAST // PAGE
EPS = 1e-6
BIG = 3e38
PAIR = 2 * KT * 128
OUTU = HALF * 128
RAW = 4
QKV_UNITS, O_UNITS = 8, 4
C_ID, C_ONE, C_CAP, C_ND, C_NDS, C_BM, C_LAST = 0, 128, 256, 704, 1088, 1408, 1416
C_COLS = 1424
R_SEL, R_HALF, R_MUL, R_NEG, R_DEL, R_M0 = 0, 1024, 1280, 1600, 1920, 1928
R_COLS = 2248
P_G, P_HEAD, P_BI, P_BF = 0, 64, 72, 73
P_COLS = 74
N_A0, N_A1, N_A2, N_KV, N_B0, N_B1, N_B2, N_FIN = range(8)


def slopes():
    return [2.0 ** (-8.0 * (h + 1) / H) for h in range(H)]


class Chain:

    def __init__(self, eng, sem):
        self.eng, self.sem, self.n, self.off = eng, sem, 0, 0

    def link(self, ins):
        self.n += 1
        ins.then_inc(self.sem, 1)
        self.eng.wait_ge(self.sem, self.n + self.off)


def trunk_program(nc, w_in, w_out, w_a, w_oa, w_kv, w_q, w_ob, w_gate, x_in, par_in, con_in, row_in,
                  c0_in, n0_in, kc_in, vc_in, pt_in,
                  y_out, k_out, v_out, cp_out, cs_out, np_out, ns_out, m_out):
    f32, f32r, i32 = mybir.dt.float32, mybir.dt.float32r, mybir.dt.int32
    ALU, ACT, AX = mybir.AluOpType, mybir.ActivationFunctionType, mybir.AxisListType
    SLOPE = slopes()
    ctx = ExitStack()
    with ctx:
        def sb(name, shape, dt=f32, where=ctx):
            return where.enter_context(nc.sbuf_tensor(name, shape, dt))

        def sem(name):
            return ctx.enter_context(nc.semaphore(name))

        raw = sb("raw", [128, RAW, PAIR])
        w_hi = sb("w_hi", [128, 2, PAIR], f32r)
        w_lo = sb("w_lo", [128, 2, PAIR], f32r)
        x = sb("x", [128, KT, T])
        h_hi = sb("h_hi", [128, KT, T], f32r)
        h_lo = sb("h_lo", [128, KT, T], f32r)
        rms = sb("rms", [128, T])
        root = sb("root", [128, T])
        sqsum = sb("sqsum", [128, T])
        sq = sb("sq", [128, 2, T])
        work = sb("work", [128, 10 * T])
        gate, up, act = (work[:, 2 * T * i:2 * T * i + 2 * T].rearrange("p (s t) -> p s t", s=2) for i in range(3))
        v_st = work[:, 6 * T:10 * T].rearrange("p (s c t) -> p s c t", s=2, c=2)
        pp = work[:, 0:768].rearrange("p (s k) -> p s k", s=2)
        pt = work[:, 768:1536].rearrange("p (s k) -> p s k", s=2)
        pn = work[0:NS, 1536:2048].rearrange("p (h t) -> p h t", h=H)
        v_tok = sb("v_tok", [128, 3, H, DV + 1])
        con = sb("con", [128, C_COLS])
        row = sb("row", [8, R_COLS])
        par = sb("par", [128, P_COLS])
        wg = sb("wg", [128, KT, 40])
        epsc = sb("epsc", [128, 1])
        pages = sb("pages", [1, NB * NPG], i32)
        mhalf = sb("mhalf", [128, 3])

        with ExitStack() as ov:
            with ExitStack() as own:
                qT = sb("qT", [128, HP, T], f32, own)
                kT = sb("kT", [128, HP, 384], f32, own)
                og = sb("og", [128, H, T], f32, own)
                kw = sb("kw", [128, 3, H * DK], f32, own)
                kwm = sb("kwm", [NS, 2, NB, DK], f32, own)
                rows = sb("rows", [128, T], f32, own)
                cols = sb("cols", [128, 3, 128], f32, own)
                g40 = sb("g40", [40, T], f32, own)
                fz = sb("fz", [8, T], f32, own)
                fa = sb("fa", [8, T], f32, own)
                cb = sb("cb", [8, T], f32, own)
                cm = sb("cm", [8, T], f32, own)
                neg = sb("neg", [8, 384], f32, own)
                mt = sb("mt", [8, T], f32, own)
                tmp = sb("tmp", [8, T], f32, own)
                mo = sb("mo", [8, 1 + NB], f32, own)
                dmat = sb("dmat", [128, 448], f32, own)
                pmat = sb("pmat", [128, 512], f32, own)
                qm = sb("qm", [128, 2, 4 * (NS + 2 * TS)], f32, own)
                c0 = sb("c0", [128, 2, 4, DV + 1], f32, own)
                cn = sb("cn", [128, 4, DV], f32, own)
                cpn = sb("cpn", [DK, DV], f32, own)
                ot = sb("ot", [128, 3, DV], f32, own)
                junk = sb("junk", [128, 3, DV], f32, own)
                ssqh, den, var, scl = (sb(n, [128, 3], f32, own) for n in ("ssqh", "den", "var", "scl"))
                ac_rhs = sb("ac_rhs", [8, 2, 4, H], f32, own)
                acb = sb("acb", [128, 4, H], f32, own)
                n0 = sb("n0", [NB, H, DK], f32, own)
                nn = sb("nn", [NB, H, DK], f32, own)
                al = sb("al", [NB, H], f32, own)
            k_all = sb("k_all", [128, H, T], f32, ov)
            with ExitStack() as own:
                f_hi = sb("f_hi", [128, FK, T], f32r, own)
                f_lo = sb("f_lo", [128, FK, T], f32r, own)
            with ExitStack() as own:
                qa = sb("qa", [128, H, T], f32, own)
                spread0 = sb("spread0", [128, H, NB * (NS + TS)], f32, own)
                spread1 = sb("spread1", [128, H, NB * (NS + TS)], f32, own)
                ss = sb("ss", [NS, H, PAST + NS], f32, own)
                st = sb("st", [128, 2, 6], f32, own)
                sst = sb("sst", [NS, 3, H], f32, own)

        npp = pmat[0:1, :]
        o_rows = qa[0:NS, :, :].rearrange("p h t -> p (h t)")[:, 0:H * DV]
        ident, ones = con[:, C_ID:C_ID + 128], con[:, C_ONE:C_ONE + 128]
        sel = row[:, R_SEL:R_SEL + 1024].rearrange("k (h p) -> k h p", h=H)
        bank = [ctx.enter_context(nc.psum_tensor(f"bank{i}", [128, 512], f32)) for i in range(8)]

        s_con = sem("constants_loaded")
        s_x = [sem(f"x_loaded{m}") for m in range(KT)]
        s_n0 = sem("state_n_loaded")
        s_pg = sem("page_table_loaded")
        s_set = sem("eps_set")
        loaded = [sem(f"raw_loaded{i}") for i in range(RAW)]
        hi_done = sem("weight_hi_done")
        lo_done = sem("weight_lo_done")
        unit_done = sem("unit_multiplied")
        kv_used = sem("cache_unit_used")
        pair_free = sem("pair_banks_evacuated")
        gate_ready = sem("gate_scaled")
        silu_ready = sem("silu_done")
        hid_ready = sem("hidden_done")
        hid_hi = sem("hidden_hi_done")
        hid_lo = sem("hidden_lo_done")
        x_ready = sem("x_chunk_ready")
        hh_done = sem("h_hi_done")
        hl_done = sem("h_lo_done")
        sq_done = sem("squares_done")
        sum_done = sem("square_sum_done")
        ssq_done = sem("square_total_done")
        root_done = sem("root_done")
        rms_done = sem("rms_done")
        s_dve = sem("vector_steps")
        s_act = sem("scalar_steps")
        s_out = sem("outputs_stored")
        s_y = sem("y_stored")
        y_done = sem("y_chunk_done")
        mo_done = sem("last_m_gathered")
        spread_set = sem("spread_zeros_set")
        sm_tn = sem("sample_new_probs_copied")
        cp_out_s = sem("prompt_state_stored")
        gates_mm = sem("gates_multiplied")
        wgg_done = sem("gate_weights_scaled")
        abs_done = sem("gate_abs_done")
        ln_done = sem("gate_log_done")
        dm_done = sem("m0_minus_m_done")
        mt_done = sem("m_rows_done")
        aw_done = sem("key_weight_rows_done")
        rows_a = sem("rows_by_vector_done")
        rows_b = sem("rows_by_scalar_done")
        rows_t = sem("rows_transposed")
        cols_done = sem("columns_done")
        ac_done = sem("carry_factors_done")
        acb_mm = sem("carry_factors_spread")
        o_even = sem("output_gate_even_chunk_multiplied")
        o_kept = sem("output_gate_chunk_kept")
        tanh_done = sem("output_gate_tanh_done")
        og_done = sem("output_gate_done")
        tr_done = sem("transposes_done")
        tr_free = sem("transposes_evacuated")
        kt_tr = sem("keys_transposed")
        kw_done = sem("weighted_keys_done")
        zero_done = sem("zeros_set")
        head_s = sem("head_scores_done")
        d_done = sem("head_decay_done")
        w_done = sem("head_weights_done")
        p_done = sem("head_products_done")
        qm_done = sem("head_queries_spread")
        kwm_done = sem("head_keys_spread")
        c0_load = [sem("state_c_loaded0"), sem("state_c_loaded1")]
        head_o = sem("head_outputs_done")
        cp_done = sem("prompt_state_copied")
        cn_done = sem("sample_state_done")
        cn_out = sem("sample_state_stored")
        den_done = sem("head_denominators_read")
        ssq_h = sem("head_squares_done")
        s_in = sem("head_scale_in_done")
        s_pow = sem("head_scale_done")
        ot_done = sem("head_scaled")
        ot_tr = sem("head_transposed")
        z_done = sem("head_gated")
        n_mm = sem("n_multiplied")
        n_done = sem("n_done")
        qa_sp = sem("queries_spread")
        new_s = sem("new_scores_done")
        pr_s = sem("prompt_scores_done")
        pr_b = sem("prompt_scores_biased")
        pr_m = sem("prompt_max_done")
        pr_e = sem("prompt_exp_done")
        pr_p = sem("prompt_probs_done")
        pr_t = sem("prompt_probs_transposed")
        pr_tc = sem("prompt_probs_copied")
        pr_o = sem("prompt_outputs_done")
        pr_hi = sem("prompt_outputs_hi")
        pr_lo = sem("prompt_outputs_lo")
        sm_m = sem("sample_max_done")
        sm_e = sem("sample_exp_done")
        sm_p = sem("sample_probs_done")
        sm_t = sem("sample_probs_transposed")
        sm_tc = sem("sample_probs_spread")
        sm_o = sem("sample_outputs_done")
        sm_oc = sem("sample_outputs_copied")
        sm_ot = sem("sample_outputs_transposed")
        sm_hi = sem("sample_outputs_hi")
        sm_lo = sem("sample_outputs_lo")

        FFN_UNITS = FK + 2 * KT
        U_FFN = [0, 0, 0, 0]
        at = 0
        U_FFN[0] = at; at += FFN_UNITS
        U_A = at; at += QKV_UNITS + O_UNITS
        U_OA = at; at += 4
        U_FFN[1] = at; at += FFN_UNITS
        U_KV = at; at += 8
        U_FFN[2] = at; at += FFN_UNITS
        U_Q = at; at += 4
        U_OB = at; at += 4
        U_FFN[3] = at; at += FFN_UNITS
        U_END = at
        CACHE = 2 * NB

        P_A = FK
        P_OA = P_A + QKV_UNITS
        P_KV = P_OA + FK
        P_Q = P_KV + 8 + FK
        P_OB = P_Q + 4
        P_FFN = [0, P_OA, P_KV + 8, P_OB]

        HALVES = {1: ((10, 0),), 2: ((10, 1),), 3: ((11, 0),), 4: ((11, 1),), 5: ((12, 0),), 6: ((12, 1),),
                  7: ((13, 0), (13, 1))}
        XB = [0, 2 * KT, 3 * KT, 5 * KT]

        block = ctx.enter_context(nc.Block())

        def loads_after(r):
            return sum(32 if U_OB <= q < U_OB + CACHE else 16 for q in range(r % RAW, r + 1, RAW))

        def raw_of(n):
            return n + (CACHE if n >= U_OB else 0)

        def width(n):
            return OUTU if any(f + FK <= n < f + FFN_UNITS for f in U_FFN) else PAIR

        @block.sync
        def _(sp):
            def load(r, src, w):
                before = r - RAW
                if 0 <= before < U_OB:
                    sp.wait_ge(lo_done, before + 1)
                elif U_OB <= before < U_OB + CACHE:
                    sp.wait_ge(kv_used, before - U_OB + 1)
                elif before >= 0:
                    sp.wait_ge(lo_done, before - CACHE + 1)
                sp.dma_start(raw[:, r % RAW, 0:w], src).then_inc(loaded[r % RAW], 16)

            def ffn(f):
                base = raw_of(U_FFN[f])
                for k in range(RAW):
                    load(base + k, w_in[f, k], PAIR)
                    if f == 0 and k == 0:
                        sp.dma_start(row[:, :], row_in).then_inc(s_con, 16)
                        sp.dma_start(wg[:, :, :], w_gate).then_inc(s_con, 16)
                        sp.dma_start(pages[:, :], pt_in).then_inc(s_pg, 16)
                with sp.Fori(0, (FK - RAW) // RAW) as i:
                    for j in range(RAW):
                        sp.wait_ge(lo_done, i * RAW + (U_FFN[f] + j + 1))
                        sp.dma_start(raw[:, (base + j) % RAW, 0:PAIR],
                                     w_in[f, bass.ds(i * RAW + (RAW + j), 1)].rearrange("a p c -> p (a c)")
                                     ).then_inc(loaded[(base + j) % RAW], 16)
                for k in range(FK - FK % RAW, FK):
                    load(base + k, w_in[f, k], PAIR)
                for k in range(2 * KT):
                    load(base + FK + k, w_out[f, k], OUTU)

            sp.dma_start(par[:, :], par_in).then_inc(s_con, 16)
            for m in range(KT):
                sp.dma_start(x[:, m, :], x_in[:, m, :]).then_inc(s_x[m], 16)
                if m == 3:
                    sp.dma_start(con[:, :], con_in).then_inc(s_con, 16)
            ffn(0)
            for k in range(QKV_UNITS + O_UNITS):
                load(U_A + k, w_a[k], PAIR)
            for k in range(4):
                load(U_OA + k, w_oa[k], PAIR)
            ffn(1)
            for k in range(8):
                load(U_KV + k, w_kv[k], PAIR)
            ffn(2)
            for k in range(4):
                load(U_Q + k, w_q[k], PAIR)
            sp.wait_ge(s_pg, 16)
            for kind, src in enumerate((kc_in, vc_in)):
                for b in range(NB):
                    r = U_OB + kind * NB + b
                    if r - RAW < U_OB:
                        sp.wait_ge(lo_done, r - RAW + 1)
                    else:
                        sp.wait_ge(kv_used, r - RAW - U_OB + 1)
                    for pg in range(NPG):
                        page = sp.value_load(pages[0:1, b * NPG + pg:b * NPG + pg + 1], min_val=0,
                                             max_val=kc_in.shape[0] - 1)
                        sp.dma_start(raw[:, r % RAW, pg * 1024:pg * 1024 + 1024],
                                     src[bass.ds(page, 1)].rearrange("a p c -> p (a c)")
                                     ).then_inc(loaded[r % RAW], 16)
            for k in range(4):
                load(U_OB + CACHE + k, w_ob[k], PAIR)
            ffn(3)
            for m in range(KT):
                sp.wait_ge(y_done, m + 1)
                sp.dma_start(y_out[:, m, :], x[:, m, :]).then_inc(s_y, 16)
            sp.wait_ge(s_y, 16 * KT)
            sp.wait_ge(cn_out, 16 * H)
            sp.wait_ge(cp_out_s, 16 * H)
            sp.wait_ge(s_out, 16 * 5)

        @block.tensor
        def _(pe):
            def passes(out, wh, wl, mh, ml, first, last):
                pe.matmul(out, wh, mh, start=first, stop=False)
                pe.matmul(out, wh, ml, start=False, stop=False)
                return pe.matmul(out, wl, mh, start=False, stop=last)

            def chunk(out, s, c, h_wait):
                for kt in range(KT):
                    if h_wait is not None:
                        pe.wait_ge(hl_done, h_wait + kt + 1)
                    w = (c * KT + kt) * 128
                    mm = passes(out, w_hi[:, s, w:w + 128], w_lo[:, s, w:w + 128],
                                h_hi[:, kt, :], h_lo[:, kt, :], kt == 0, kt == KT - 1)
                return mm

            def pair_unit(n, p, n_at, p_at, h_wait=None, between=None, added=None):
                pe.wait_ge(lo_done, n + 1)
                if added:
                    pe.wait_ge(x_ready, added)
                elif p_at >= 2:
                    pe.wait_ge(pair_free, p - 1)
                b = 2 * (p_at % 2)
                chunk(bank[b][:, 0:T], n_at % 2, 0, h_wait)
                if between:
                    between()
                chunk(bank[b + 1][:, 0:T], n_at % 2, 1, None).then_inc(unit_done, 1)

            def units(u, p, first, end, **kw0):
                for k in range(first, end):
                    pair_unit(u + k, p + k, u + k, p + k, **(kw0 if k == first else {}))

            def units_to_x(u, p, xbase, first, end, h_wait=None):
                for k in range(first, end):
                    pair_unit(u + k, p + k, u + k, p + k, h_wait if k == 0 else None,
                              added=xbase + 2 * k - 2 if k >= 2 else None)

            def total(j):
                pe.wait_ge(sum_done, KT * (j + 1))
                if j >= 1:
                    pe.wait_ge(root_done, j)
                pe.matmul(bank[6][:, 0:T], ones, sqsum[:, :], start=True, stop=True).then_inc(ssq_done, 1)

            def ffn(f, h_wait, between):
                u, p = U_FFN[f], P_FFN[f]
                pair_unit(u, p, u, p, h_wait, between)
                units(u, p, 1, 3)
                with pe.Fori(0, (FK - 4) // 2) as i:
                    for j in (3, 4):
                        pair_unit(i * 2 + (u + j), i * 2 + (p + j), u + j, p + j)
                pair_unit(u + FK - 1, p + FK - 1, u + FK - 1, p + FK - 1)

                def out_chunk(m, m_at, wait_hidden):
                    out = bank[4 + m_at % 2][:, 0:T]
                    if m_at >= 2:
                        pe.wait_ge(x_ready, m + (XB[f] - 1))
                    for part in range(2):
                        pe.wait_ge(lo_done, m * 2 + (u + FK + part + 1))
                        s = (u + FK + part) % 2
                        for kt in range(HALF):
                            g = part * HALF + kt
                            if wait_hidden:
                                pe.wait_ge(hid_lo, FK * f + g + 1)
                            mm = passes(out, w_hi[:, s, kt * 128:kt * 128 + 128],
                                        w_lo[:, s, kt * 128:kt * 128 + 128],
                                        f_hi[:, g, :], f_lo[:, g, :], g == 0, g == FK - 1)
                        mm.then_inc(unit_done, 1)

                out_chunk(0, 0, True)
                out_chunk(1, 1, False)
                with pe.Fori(0, (KT - 2) // 2) as i:
                    for j in (2, 3):
                        out_chunk(i * 2 + j, j, False)

            groups = [0]

            def turn_values(p, v_unit):
                pe.wait_ge(pair_free, p + 1)
                for c in range(2):
                    g = groups[0]
                    groups[0] += 1
                    if g >= 2:
                        pe.wait_ge(tr_free, g - 1)
                    for t in range(3):
                        w = 128 if t < 2 else NS
                        mm = pe.transpose(bank[4 + g % 2][0:w, t * 128:t * 128 + 128],
                                          v_st[:, v_unit % 2, c, t * 128:t * 128 + w], ident)
                    mm.then_inc(tr_done, 1)

            pe.wait_ge(s_con, 64)
            ffn(0, 0, lambda: total(0))

            def gates():
                total(1)
                pe.wait_ge(wgg_done, KT)
                for kt in range(KT):
                    mm = pe.matmul(bank[7][0:40, 0:T], wg[:, kt, :], x[:, kt, :],
                                   start=(kt == 0), stop=(kt == KT - 1))
                mm.then_inc(gates_mm, 1)

            def turn_rows():
                pe.wait_ge(rows_a, 1)
                pe.wait_ge(rows_b, 4)
                for t in range(3):
                    w = 128 if t < 2 else NS
                    mm = pe.transpose(bank[6][0:w, t * 128:t * 128 + 128], rows[:, t * 128:t * 128 + w], ident)
                mm.then_inc(rows_t, 1)
                pe.wait_ge(ac_done, 2)
                for half in range(2):
                    mm = pe.matmul(bank[7][:, 0:32], row[:, R_HALF + 128 * half:R_HALF + 128 * half + 128],
                                   ac_rhs[:, half, :, :].rearrange("k a h -> k (a h)"),
                                   start=(half == 0), stop=(half == 1))
                mm.then_inc(acb_mm, 1)

            def turn_keys(t):
                if t < 2:
                    pe.wait_ge(cols_done, 3)
                else:
                    pe.wait_ge(kw_done, t - 1)
                w = 128 if t < 2 else NS
                for hp in range(HP):
                    mm = pe.transpose(bank[6 + t % 2][0:w, hp * 128:hp * 128 + 128],
                                      kT[:, hp, t * 128:t * 128 + w], ident)
                mm.then_inc(kt_tr, 1)

            def o_chunk(c):
                u = U_A + QKV_UNITS + c // 2
                pe.wait_ge(lo_done, u + 1)
                if c < 2:
                    pe.wait_ge(pair_free, P_A + QKV_UNITS - 1)
                else:
                    pe.wait_ge(o_kept, c - 1)
                chunk(bank[c % 2][:, 0:T], u % 2, c % 2, None).then_inc(unit_done if c % 2 else o_even, 1)

            def head_scores(h):
                hp, r = h // 2, slice(64 * (h % 2), 64 * (h % 2) + 64)
                if h == 0:
                    pe.wait_ge(pair_free, P_A + 7)
                    pe.wait_ge(tr_free, 8)
                else:
                    pe.wait_ge(pair_free, P_A + 8)
                    pe.wait_ge(qm_done, 2 * h)
                    pe.wait_ge(p_done, h)
                pe.matmul(bank[4][:, 0:384], sel[:, h, :], neg[:, :], start=True, stop=True)
                pe.matmul(bank[5][:, 0:256], kT[r, hp, 0:128], qT[r, hp, 0:256], start=True, stop=True)
                pe.matmul(bank[5][:, 256:384], kT[r, hp, 128:256], qT[r, hp, 128:256], start=True, stop=True)
                pe.matmul(bank[5][:, 384:448], kT[r, hp, 256:384], qT[r, hp, 256:320],
                          start=True, stop=True).then_inc(head_s, 1)

            def head_outputs(h):
                W = DV + 1
                o = bank[6]
                pe.wait_ge(p_done, h + 1)
                pe.wait_ge(qm_done, 2 * h + 2)
                pe.wait_ge(c0_load[h % 2], 16 * (h // 2 + 1))
                pe.wait_ge(kwm_done, h + 1)
                if h == 0:
                    pe.wait_ge(kw_done, 3)
                    pe.wait_ge(pair_free, P_A + 8)
                else:
                    pe.wait_ge(ot_done, 3 * h)
                    pe.wait_ge(cp_done, h)
                    pe.wait_ge(cn_done, h)
                pe.matmul(o[:, 0:W], pmat[:, 0:128], v_tok[:, 0, h, :], start=True, stop=True)
                pe.matmul(o[:, W:2 * W], pmat[:, 128:256], v_tok[:, 0, h, :], start=True, stop=False)
                pe.matmul(o[:, W:2 * W], pmat[:, 256:384], v_tok[:, 1, h, :], start=False, stop=True)
                pe.matmul(o[:, 2 * W:3 * W], pmat[0:64, 384:512], v_tok[0:64, 2, h, :], start=True, stop=True)
                for a in range(4):
                    pe.matmul(o[0:64, 2 * W:3 * W], qm[:, h % 2, a * NS:a * NS + NS], c0[:, h % 2, a, :],
                              start=False, stop=(a == 3), skip_group_check=True)
                for t in range(2):
                    pe.matmul(bank[2][0:64, 0:DV], kw[:, t, h * 64:h * 64 + 64], v_tok[:, t, h, 0:DV],
                              start=(t == 0), stop=(t == 1))
                for a in range(4):
                    mm = pe.matmul(bank[7][:, a * 128:a * 128 + 128],
                                   kwm[:, h % 2, 2 * a:2 * a + 2, :].rearrange("t b d -> t (b d)"),
                                   v_tok[0:64, 2, h, 0:DV], start=True, stop=True)
                mm.then_inc(head_o, 1)

            def head_turn(h):
                pe.wait_ge(ot_done, 3 * h + 3)
                if h >= 1:
                    pe.wait_ge(z_done, h)
                for t in range(3):
                    w = 128 if t < 2 else NS
                    mm = pe.transpose(bank[3][:, t * 128:t * 128 + w], ot[0:w, t, :], ident[0:w, 0:w])
                mm.then_inc(ot_tr, 1)

            units(U_A, P_A, 0, 1, h_wait=KT, between=gates)
            pe.wait_ge(x_ready, KT)
            units(U_A, P_A, 1, 4)
            turn_values(P_A + 2, 0)
            units(U_A, P_A, 4, 5)
            turn_values(P_A + 3, 1)
            units(U_A, P_A, 5, 6)
            turn_values(P_A + 4, 2)
            turn_rows()
            units(U_A, P_A, 6, 7)
            turn_values(P_A + 5, 3)
            turn_keys(0)
            turn_keys(1)

            def first_scores():
                turn_keys(2)
                head_scores(0)

            units(U_A, P_A, 7, 8, between=first_scores)
            o_chunk(0)
            for h in range(H):
                head_outputs(h)
                if h + 1 < H:
                    head_scores(h + 1)
                    o_chunk(h + 1)
                else:
                    pe.wait_ge(p_done, H)
                    for t in range(2):
                        pe.matmul(bank[4][0:1, :], ones[:, 0:1], kw[:, t, :], start=(t == 0), stop=(t == 1))
                    pe.matmul(bank[5][0:8, 0:8], con[0:64, C_LAST:C_LAST + 8], cols[0:64, 2, 64:72],
                              start=True, stop=True)
                head_turn(h)
            pe.matmul(bank[6][0:8, :], con[0:64, C_BM:C_BM + 8], kw[0:64, 2, :],
                      start=True, stop=True).then_inc(n_mm, 1)
            pe.wait_ge(cp_done, H)
            units_to_x(U_OA, P_OA, KT, 0, 4, 2 * KT)
            pe.wait_ge(n_done, 2)
            ffn(1, 3 * KT, lambda: total(2))

            units(U_KV, P_KV, 0, 1, h_wait=4 * KT, between=lambda: total(3))
            pe.wait_ge(x_ready, 3 * KT)
            for k in range(1, 8):
                units(U_KV, P_KV, k, k + 1)
                if k >= 5:
                    turn_values(P_KV + k - 1, k - 5)

            def last_values():
                turn_values(P_KV + 7, 3)
                pe.wait_ge(tr_free, 16)

            ffn(2, 5 * KT, last_values)
            units(U_Q, P_Q, 0, 1, h_wait=6 * KT, between=lambda: total(4))
            units(U_Q, P_Q, 1, 4)

            def prompt_scores(h):
                if h >= 1:
                    pe.wait_ge(pr_b, h)
                pe.matmul(bank[5][:, 0:128], qa[:, h, 0:128], k_all[:, h, 0:128], start=True, stop=True)
                pe.matmul(bank[5][:, 128:384], qa[:, h, 128:256], k_all[:, h, 0:256],
                          start=True, stop=True).then_inc(pr_s, 1)

            def prompt_turn(h):
                pe.wait_ge(pr_p, h + 1)
                if h >= 1:
                    pe.wait_ge(pr_tc, h)
                for i in range(3):
                    mm = pe.transpose(bank[6][:, i * 128:i * 128 + 128],
                                      pp[:, h % 2, i * 128:i * 128 + 128], ident)
                mm.then_inc(pr_t, 1)

            def prompt_outputs(h):
                pe.wait_ge(pr_tc, h + 1)
                if h >= 1:
                    pe.wait_ge(pr_lo, h)
                pe.matmul(bank[7][:, 0:256], v_tok[:, 0, h, 0:DV], pt[:, h % 2, 0:256], start=True, stop=False)
                pe.matmul(bank[7][:, 128:256], v_tok[:, 1, h, 0:DV], pt[:, h % 2, 256:384],
                          start=False, stop=True).then_inc(pr_o, 1)

            pe.wait_ge(pair_free, P_Q + 4)
            pe.wait_ge(x_ready, 4 * KT)
            for h in range(H):
                mm = pe.matmul(bank[4][0:NS, h * NS:h * NS + NS], qa[:, h, TP:T], k_all[:, h, TP:T],
                               start=True, stop=True)
            mm.then_inc(new_s, 1)
            pe.wait_ge(qa_sp, 1)
            for b in range(NB):
                r = U_OB + b
                pe.wait_ge(loaded[r % RAW], loads_after(r))
                for h in range(H):
                    keys = raw[:, r % RAW, :].rearrange("p (g h s) -> p g h s", g=NPG, h=H)[:, :, h, :]
                    mm = pe.matmul(bank[h // 2][0:NS, (h % 2) * PAST:(h % 2) * PAST + PAST],
                                   spread0[:, h, b * NS:b * NS + NS], keys,
                                   start=(b == 0 and h % 2 == 0), stop=(b == NB - 1), skip_group_check=True)
                mm.then_inc(kv_used, 1)
                if b >= 1:
                    prompt_turn(b - 1)
                prompt_scores(b)
                if b >= 1:
                    prompt_outputs(b - 1)
            prompt_turn(NB - 1)
            prompt_outputs(NB - 1)

            pe.wait_ge(sm_p, H)
            for g in range(NPG):
                for h in range(H):
                    mm = pe.transpose(bank[g][:, h * NS:h * NS + NS], ss[:, h, g * PAGE:g * PAGE + PAGE],
                                      ident[0:NS, 0:NS])
                mm.then_inc(sm_t, 1)
            for h in range(H):
                mm = pe.transpose(bank[4][0:NS, h * NS:h * NS + NS], ss[:, h, PAST:PAST + NS],
                                  ident[0:NS, 0:NS])
            mm.then_inc(sm_t, 1)
            pe.wait_ge(sm_tn, 1)
            for h in range(H):
                pe.matmul(bank[2 + h // 4][0:NS, (h % 4) * 128:(h % 4) * 128 + 128], pn[:, h, :],
                          v_tok[0:NS, 2, h, 0:DV], start=(h % 4 == 0), stop=False, skip_group_check=True)
            pe.wait_ge(sm_tc, 2)
            for b in range(NB):
                r = U_OB + NB + b
                pe.wait_ge(loaded[r % RAW], loads_after(r))
                for g, spread in enumerate((spread0, spread1)):
                    for h in range(H):
                        v = g * 1024 + h * 128
                        mm = pe.matmul(bank[2 + h // 4][0:NS, (h % 4) * 128:(h % 4) * 128 + 128],
                                       spread[:, h, b * NS:b * NS + NS], raw[:, r % RAW, v:v + 128],
                                       start=False, stop=(b == NB - 1 and g == 1), skip_group_check=True)
                mm.then_inc(kv_used, 1)
            pe.wait_ge(sm_oc, 2)
            for h in range(H):
                mm = pe.transpose(bank[0][:, h * NS:h * NS + NS], o_rows[:, h * 128:h * 128 + 128],
                                  ident[0:NS, 0:NS])
            mm.then_inc(sm_ot, 1)

            pe.wait_ge(pr_lo, H)
            pe.wait_ge(sm_lo, 1)
            units_to_x(U_OB, P_OB, 4 * KT, 0, 4)
            ffn(3, 7 * KT, lambda: total(5))
            total(6)

        @block.scalar
        def _(sc):
            chain = Chain(sc, s_act)

            def split(n, n_at, r_val):
                for part in range(2):
                    split_half(n, n_at, r_val, part)

            def split_half(n, n_at, r_val, part):
                w = width(n_at) // 2
                if part == 0:
                    sc.wait_ge(loaded[raw_of(n_at) % RAW], r_val)
                    if n_at >= 2:
                        sc.wait_ge(unit_done, n - 1)
                sc.activation(w_hi[:, n_at % 2, part * w:part * w + w],
                              raw[:, raw_of(n_at) % RAW, part * w:part * w + w], ACT.Copy).then_inc(hi_done, 1)

            def split_at(n):
                if n < U_END:
                    split(n, n, loads_after(raw_of(n)))

            def update(j, m, norm, xr):
                sc.wait_ge(*xr)
                if norm is not None:
                    h_split(m, norm)
                square(j, m)

            def square(j, m):
                c = KT * j + m
                if c >= 2:
                    sc.wait_ge(sum_done, c - 1)
                sc.activation(sq[:, m % 2, :], x[:, m, :], ACT.Square).then_inc(sq_done, 1)

            def h_split(m, norm):
                sc.activation(h_hi[:, m, :], x[:, m, :], ACT.Copy,
                              scale=par[:, P_G + KT * norm + m:P_G + KT * norm + m + 1]).then_inc(hh_done, 1)

            def root_of(j):
                sc.wait_ge(ssq_done, j + 1)
                if j >= 1:
                    sc.wait_ge(rms_done, j)
                sc.activation(root[:, :], bank[6][:, 0:T], ACT.Sqrt, bias=epsc[:, 0:1], scale=1.0 / D
                              ).then_inc(root_done, 1)

            def hidden(f, k, k_at):
                c = k + FK * f
                sc.wait_ge(gate_ready, c + 1)
                sc.activation(act[:, k_at % 2, :], gate[:, k_at % 2, :], ACT.Silu).then_inc(silu_ready, 1)
                sc.wait_ge(hid_ready, c + 1)
                dst = f_hi[:, k, :] if isinstance(k, int) else \
                    f_hi[:, bass.ds(k, 1), :].rearrange("p a t -> p (a t)")
                sc.activation(dst, up[:, k_at % 2, :], ACT.Copy).then_inc(hid_hi, 1)

            def ffn(f, j_out, norm, post, xbase):
                u = U_FFN[f]
                split_at(u + 1)
                post()
                with sc.Fori(0, (FK - 2) // 4) as i:
                    for j in range(1, 5):
                        n = u + j + 1
                        split(i * 4 + n, n, i * 16 + loads_after(raw_of(n)))
                        hidden(f, i * 4 + (j - 1), j - 1)
                split_at(u + FK)
                hidden(f, FK - 2, FK - 2)
                split_at(u + FK + 1)
                hidden(f, FK - 1, FK - 1)
                split_at(u + FK + 2)
                for m in range(1, KT):
                    split_at(u + FK + 2 * m + 1)
                    update(j_out, m - 1, norm, (x_ready, xbase + m))
                    split_at(u + FK + 2 * m + 2)

            sc.wait_ge(s_con, 16)
            for m in range(KT):
                update(0, m, N_A0, (s_x[m], 16))
            split_at(0)
            sc.wait_ge(s_set, 4)
            ffn(0, 1, N_A1, lambda: root_of(0), 0)

            def copy_values(count):
                for c in range(2):
                    g = count * 2 + c
                    h = g % H
                    b = bank[4 + g % 2]
                    sc.wait_ge(tr_done, g + 1)
                    sc.activation(v_tok[:, 0:2, h, 0:DV], b[:, 0:256].rearrange("p (t d) -> p t d", t=2), ACT.Copy)
                    sc.activation(v_tok[0:NS, 2, h, 0:DV], b[0:NS, 256:384], ACT.Copy).then_inc(tr_free, 1)

            def tanh(c):
                sc.wait_ge(o_kept, c + 1)
                sc.activation(og[:, c, :], og[:, c, :], ACT.Tanh, scale=0.5).then_inc(tanh_done, 1)

            split_at(U_A + 1)
            update(1, KT - 1, N_A1, (x_ready, KT))
            root_of(1)
            split_at(U_A + 2)
            sc.wait_ge(abs_done, 1)
            chain.link(sc.activation(fa[:, :], fa[:, :], ACT.Exp, scale=-1.0))
            sc.activation(fa[:, :], fa[:, :], ACT.Ln, bias=1.0).then_inc(ln_done, 1)
            split_at(U_A + 3)
            split_at(U_A + 4)
            sc.wait_ge(zero_done, 4)
            sc.wait_ge(dm_done, 1)
            sc.activation(rows[64:72, :], fa[:, :], ACT.Exp).then_inc(rows_b, 1)
            sc.activation(neg[:, T:384], fa[:, TP:T], ACT.Exp).then_inc(rows_b, 1)
            sc.wait_ge(mt_done, 1)
            sc.activation(rows[96:104, :], mt[:, :], ACT.Exp, scale=-1.0).then_inc(rows_b, 1)
            sc.wait_ge(aw_done, 2)
            sc.activation(rows[32:40, :], g40[0:8, :], ACT.Exp).then_inc(rows_b, 1)
            split_at(U_A + 5)
            copy_values(0)
            split_at(U_A + 6)
            copy_values(1)
            split_at(U_A + 7)
            copy_values(2)
            sc.wait_ge(rows_t, 1)
            sc.activation(cols[:, 0:2, :], bank[6][:, 0:256].rearrange("p (t r) -> p t r", t=2), ACT.Copy
                          ).then_inc(cols_done, 1)
            sc.activation(cols[0:NS, 2, :], bank[6][0:NS, 256:384], ACT.Copy).then_inc(cols_done, 1)
            sc.wait_ge(acb_mm, 1)
            sc.activation(acb[:, :, :], bank[7][:, 0:32].rearrange("p (a h) -> p a h", a=4), ACT.Copy
                          ).then_inc(cols_done, 1)
            split_at(U_A + 8)
            copy_values(3)

            def decay(h):
                sc.wait_ge(d_done, h + 1)
                sc.activation(dmat[:, :], dmat[:, :], ACT.Exp).then_inc(w_done, 1)

            def head_tail(h):
                sc.wait_ge(head_o, h + 1)
                if h >= 1:
                    sc.wait_ge(cp_out_s, 16 * h)
                sc.activation(cpn[:, :], bank[2][0:DK, 0:DV], ACT.Copy).then_inc(cp_done, 1)
                sc.wait_ge(den_done, h + 1)
                for t in range(3):
                    sc.activation(junk[:, t, :], bank[6][:, t * (DV + 1):t * (DV + 1) + DV], ACT.Square,
                                  accum_out=ssqh[:, t:t + 1]).then_inc(ssq_h, 1)
                sc.wait_ge(s_pow, h + 1)
                if h >= 1:
                    sc.wait_ge(ot_tr, h)
                for t in range(3):
                    sc.activation(ot[:, t, :], bank[6][:, t * (DV + 1):t * (DV + 1) + DV], ACT.Copy,
                                  scale=scl[:, t:t + 1]).then_inc(ot_done, 1)

            def z_split(h):
                sc.wait_ge(z_done, h + 1)
                sc.activation(h_hi[:, h, :], og[:, h, :], ACT.Copy).then_inc(hh_done, 1)

            decay(0)
            split_at(U_A + 9)
            tanh(0)
            for h in range(H):
                head_tail(h)
                if h + 1 < H:
                    decay(h + 1)
                else:
                    sc.wait_ge(unit_done, U_OA)
                    for g in range(H):
                        z_split(g)
                for k, part in HALVES.get(h, ()):
                    split_half(U_A + k, U_A + k, loads_after(U_A + k), part)
                if h + 1 < H:
                    tanh(h + 1)
            split_at(U_OA + 2)
            for k in range(3):
                for c in range(2):
                    update(2, 2 * k + c, None, (x_ready, KT + 2 * k + c + 1))
                if k < 2:
                    split_at(U_OA + 3 + k)

            def resplit(norm, n):
                sc.wait_ge(unit_done, n + 1)
                for m in range(KT):
                    h_split(m, norm)

            def after_oa():
                sc.wait_ge(x_ready, 2 * KT)
                resplit(N_A2, U_OA + 3)
                square(2, 6)
                square(2, 7)
                root_of(2)
                sc.wait_ge(s_out, 16 * 3)
                sc.wait_ge(cn_out, 16 * H)
                sc.wait_ge(cp_out_s, 16 * H)

            ffn(1, 3, N_KV, after_oa, 2 * KT)

            split_at(U_KV + 1)
            update(3, KT - 1, N_KV, (x_ready, 3 * KT))
            root_of(3)
            for k in range(1, 8):
                split_at(U_KV + k + 1)
                if k >= 6:
                    copy_values(k - 2)

            def after_kv():
                resplit(N_B0, U_KV + 7)
                copy_values(6)
                copy_values(7)

            ffn(2, 4, N_B1, after_kv, 3 * KT)

            split_at(U_Q + 1)
            update(4, KT - 1, N_B1, (x_ready, 4 * KT))
            root_of(4)
            split_at(U_Q + 2)
            split_at(U_Q + 3)

            def prompt_exp(h):
                sc.wait_ge(pr_m, 2 * h + 2)
                if h >= 2:
                    sc.wait_ge(pr_p, h - 1)
                for c, i in ((slice(0, 128), 0), (slice(128, 384), 1)):
                    sc.activation(pp[:, h % 2, c], pp[:, h % 2, c], ACT.Exp, bias=st[:, h % 2, i:i + 1],
                                  accum_out=st[:, h % 2, 2 + i:3 + i]).then_inc(pr_e, 1)

            def prompt_copy(h):
                sc.wait_ge(pr_t, h + 1)
                if h >= 2:
                    sc.wait_ge(pr_o, h - 1)
                sc.activation(pt[:, h % 2, :], bank[6][:, 0:384], ACT.Copy).then_inc(pr_tc, 1)

            def prompt_hi(h):
                sc.wait_ge(pr_o, h + 1)
                sc.activation(h_hi[:, h, 0:TP], bank[7][:, 0:TP], ACT.Copy).then_inc(pr_hi, 1)

            for b in range(NB):
                if b >= 1:
                    prompt_copy(b - 1)
                prompt_exp(b)
                if b >= 1:
                    prompt_hi(b - 1)
            prompt_copy(NB - 1)
            prompt_hi(NB - 1)
            for h in range(H):
                sc.wait_ge(sm_m, h + 1)
                sc.activation(ss[:, h, :], ss[:, h, :], ACT.Exp, bias=sst[:, 0, h:h + 1],
                              accum_out=sst[:, 1, h:h + 1]).then_inc(sm_e, 1)
            sc.wait_ge(sm_t, 3)
            sc.activation(pn[:, :, :], bank[4][0:NS, :].rearrange("p (h t) -> p h t", h=H), ACT.Copy
                          ).then_inc(sm_tn, 1)
            split_at(U_OB)
            split_at(U_OB + 1)
            sc.wait_ge(kv_used, CACHE)
            for c in range(2):
                sc.activation(o_rows[:, c * 512:c * 512 + 512], bank[2 + c][0:NS, :], ACT.Copy
                              ).then_inc(sm_oc, 1)
            sc.wait_ge(sm_ot, 1)
            sc.activation(h_hi[:, :, TP:T], bank[0][:, :].rearrange("p (h t) -> p h t", h=H), ACT.Copy
                          ).then_inc(sm_hi, 1)
            for k in range(3):
                split_at(U_OB + 2 + k)
                for c in range(2):
                    update(5, 2 * k + c, None, (x_ready, 4 * KT + 2 * k + c + 1))

            def after_ob():
                sc.wait_ge(x_ready, 5 * KT)
                resplit(N_B2, U_OB + 3)
                square(5, 6)
                square(5, 7)
                root_of(5)

            ffn(3, 6, None, after_ob, 5 * KT)
            update(6, KT - 1, None, (x_ready, 6 * KT))
            root_of(6)

        @block.vector
        def _(ve):
            chain = Chain(ve, s_dve)

            def split(n, n_at):
                split_half(n, n_at, 0)
                split_half(n, n_at, 1)

            def split_half(n, n_at, part):
                w = width(n_at) // 2
                c = slice(part * w, part * w + w)
                ve.wait_ge(hi_done, n * 2 + (part + 1))
                ins = ve.tensor_tensor(w_lo[:, n_at % 2, c], raw[:, raw_of(n_at) % RAW, c],
                                       w_hi[:, n_at % 2, c].bitcast(f32), ALU.subtract)
                if part:
                    ins.then_inc(lo_done, 1)

            def split_at(n):
                if n < U_END:
                    split(n, n)

            def h_lo_of(m, norm, count):
                ve.wait_ge(hh_done, count)
                ve.scalar_tensor_tensor(out=h_lo[:, m, :], in0=x[:, m, :],
                                        scalar=par[:, P_G + KT * norm + m:P_G + KT * norm + m + 1],
                                        in1=h_hi[:, m, :].bitcast(f32), op0=ALU.mult, op1=ALU.subtract
                                        ).then_inc(hl_done, 1)

            def rms_of(j):
                ve.wait_ge(root_done, j + 1)
                ve.reciprocal(rms[:, :], root[:, :]).then_inc(rms_done, 1)
                ve.wait_ge(rms_done, j + 1)

            def scaled(f, k, k_at, p):
                b = 2 * ((P_FFN[f] + k_at) % 2)
                ve.wait_ge(unit_done, k + (U_FFN[f] + 1))
                ve.tensor_tensor(gate[:, k_at % 2, :], bank[b][:, 0:T], rms[:, :], ALU.mult).then_inc(gate_ready, 1)
                ve.tensor_tensor(up[:, k_at % 2, :], bank[b + 1][:, 0:T], rms[:, :], ALU.mult).then_inc(pair_free, 1)

            def hidden(f, k, k_at):
                c = k + FK * f
                ve.wait_ge(pair_free, k + (P_FFN[f] + 1))
                ve.wait_ge(silu_ready, c + 1)
                ve.tensor_tensor(up[:, k_at % 2, :], up[:, k_at % 2, :], act[:, k_at % 2, :], ALU.mult
                                 ).then_inc(hid_ready, 1)
                ve.wait_ge(hid_hi, c + 1)
                if isinstance(k, int):
                    hi, lo = f_hi[:, k, :], f_lo[:, k, :]
                else:
                    hi, lo = (t[:, bass.ds(k, 1), :].rearrange("p a t -> p (a t)") for t in (f_hi, f_lo))
                ve.tensor_tensor(lo, up[:, k_at % 2, :], hi.bitcast(f32), ALU.subtract).then_inc(hid_lo, 1)

            def add_out(f, m):
                ve.wait_ge(unit_done, U_FFN[f] + FK + 2 * m + 2)
                ve.scalar_tensor_tensor(out=x[:, m, :], in0=bank[4 + m % 2][:, 0:T], scalar=0.5,
                                        in1=x[:, m, :], op0=ALU.mult, op1=ALU.add).then_inc(x_ready, 1)

            def add_pair(u, p, k):
                ve.wait_ge(unit_done, u + k + 1)
                b = 2 * ((p + k) % 2)
                for c in range(2):
                    ve.tensor_tensor(x[:, 2 * k + c, :], bank[b + c][:, 0:T], x[:, 2 * k + c, :], ALU.add
                                     ).then_inc(x_ready, 1)

            def ffn(f, norm, hbase, post):
                u, p = U_FFN[f], P_FFN[f]
                post()
                with ve.Fori(0, (FK - 2) // 4) as i:
                    for j in range(1, 5):
                        k, k_at = i * 4 + (j - 1), j - 1
                        scaled(f, k, k_at, p)
                        split(i * 4 + (u + j + 1), u + j + 1)
                        hidden(f, k, k_at)
                for k in (FK - 2, FK - 1):
                    scaled(f, k, k, p)
                    split_at(u + k + 2)
                    hidden(f, k, k)
                split_at(u + FK + 2)
                for m in range(1, KT):
                    add_out(f, m - 1)
                    split_at(u + FK + 2 * m + 1)
                    if norm is not None:
                        h_lo_of(m - 1, norm, hbase + m)
                    split_at(u + FK + 2 * m + 2)

            ve.wait_ge(s_con, 16)
            for m in range(KT):
                ve.wait_ge(s_x[m], 16)
                h_lo_of(m, N_A0, m + 1)
            split_at(0)
            ve.wait_ge(s_con, 64)
            for m in range(KT):
                ve.tensor_scalar(wg[:, m, :], wg[:, m, :],
                                 par[:, P_G + KT * N_A1 + m:P_G + KT * N_A1 + m + 1], None, ALU.mult
                                 ).then_inc(wgg_done, 1)

            def first_post():
                split_at(1)
                rms_of(0)

            ffn(0, N_A1, KT, first_post)

            def project(k):
                b = 2 * ((P_A + k) % 2)
                ve.wait_ge(unit_done, U_A + k + 1)
                for c in range(2):
                    src = bank[b + c][:, 0:T]
                    if k < 2:
                        ins = ve.scalar_tensor_tensor(out=kT[:, 2 * k + c, 0:T], in0=src,
                                                      scalar=DK ** -0.5, in1=rms[:, :],
                                                      op0=ALU.mult, op1=ALU.mult)
                    elif k < 6:
                        if k >= 4 and c == 0:
                            ve.wait_ge(tr_done, 2 * (k - 3))
                        ins = ve.tensor_tensor(v_st[:, k % 2, c, :], src, rms[:, :], ALU.mult)
                    else:
                        ins = ve.tensor_tensor(qT[:, 2 * (k - 6) + c, :], src, rms[:, :], ALU.mult)
                ins.then_inc(pair_free, 1)

            def keep_gate(c):
                if c % 2:
                    ve.wait_ge(unit_done, U_A + QKV_UNITS + c // 2 + 1)
                else:
                    ve.wait_ge(o_even, c // 2 + 1)
                ve.tensor_tensor(og[:, c, :], bank[c % 2][:, 0:T], rms[:, :], ALU.mult).then_inc(o_kept, 1)

            def gate_half(c):
                ve.wait_ge(tanh_done, c + 1)
                ve.tensor_scalar(og[:, c, :], og[:, c, :], 0.5, 0.5, ALU.mult, ALU.add).then_inc(og_done, 1)

            add_out(0, KT - 1)
            split_at(U_A + 1)
            h_lo_of(KT - 1, N_A1, 2 * KT)
            rms_of(1)
            project(0)
            ve.wait_ge(gates_mm, 1)
            chain.link(ve.tensor_tensor(g40[:, :], bank[7][0:40, 0:T], rms[0:40, :], ALU.mult))
            ve.tensor_scalar(tmp[:, :], g40[0:8, :], par[0:8, P_BI:P_BI + 1], None, ALU.add)
            chain.link(ve.tensor_scalar(fz[:, :], g40[32:40, :], par[32:40, P_BF:P_BF + 1], None, ALU.add))
            ve.scalar_tensor_tensor(out=fa[:, :], in0=fz[:, :], scalar=-1.0, in1=fz[:, :],
                                    op0=ALU.mult, op1=ALU.max).then_inc(abs_done, 1)
            split_at(U_A + 2)
            project(1)
            split_at(U_A + 3)
            ve.wait_ge(ln_done, 1)
            chain.link(ve.scalar_tensor_tensor(out=fz[:, :], in0=fz[:, :], scalar=0.0, in1=fa[:, :],
                                               op0=ALU.min, op1=ALU.subtract))
            chain.link(ve.tensor_tensor_scan(cb[:, :], row[:, R_MUL:R_MUL + T], fz[:, :], 0.0,
                                             ALU.mult, ALU.add))
            chain.link(ve.tensor_tensor(tmp[:, :], tmp[:, :], cb[:, :], ALU.subtract))
            chain.link(ve.tensor_tensor_scan(cm[:, :], row[:, R_NEG:R_NEG + T], tmp[:, :], 0.0,
                                             ALU.add, ALU.max))
            chain.link(ve.tensor_tensor(cm[:, :], cm[:, :], row[:, R_M0:R_M0 + T], ALU.max))
            project(2)
            split_at(U_A + 4)
            ve.tensor_scalar(neg[:, 0:T], cm[:, :], -1.0, None, ALU.mult)
            ve.tensor_tensor(fa[:, :], row[:, R_M0:R_M0 + T], cm[:, :], ALU.subtract).then_inc(dm_done, 1)
            ve.tensor_tensor(mt[:, :], cb[:, :], cm[:, :], ALU.add).then_inc(mt_done, 1)
            seqs = "k (b t) -> k b t"
            ve.tensor_scalar(g40[0:8, 0:TP], tmp[:, 0:TP], cm[:, TP - 1:TP], None, ALU.subtract
                             ).then_inc(aw_done, 1)
            ve.tensor_tensor(g40[0:8, TP:T].rearrange(seqs, b=NB), tmp[:, TP:T].rearrange(seqs, b=NB),
                             cm[:, TP:T].rearrange(seqs, b=NB)[:, :, TS - 1:TS].to_broadcast([8, NB, TS]),
                             ALU.subtract).then_inc(aw_done, 1)
            ve.wait_ge(zero_done, 4)
            ve.tensor_copy(rows[0:8, :], tmp[:, :]).then_inc(rows_a, 1)
            ve.wait_ge(mt_done, 1)
            ve.tensor_copy(mo[:, 0:1], mt[:, TP - 1:TP]).then_inc(mo_done, 1)
            ve.tensor_copy(mo[:, 1:1 + NB].unsqueeze(2), mt[:, TP:T].rearrange(seqs, b=NB)[:, :, TS - 1:TS]
                           ).then_inc(mo_done, 1)
            project(3)
            split_at(U_A + 5)
            ve.wait_ge(rows_b, 2)
            for half in range(2):
                last = neg[:, T:384].rearrange("k (a s t) -> k a s t", a=4, s=2)[:, :, half, TS - 1:TS]
                ve.tensor_tensor(ac_rhs[:, half, :, :], last.to_broadcast([8, 4, H]),
                                 row[:, R_DEL:R_DEL + 8].unsqueeze(1).to_broadcast([8, 4, H]), ALU.mult
                                 ).then_inc(ac_done, 1)
            project(4)
            split_at(U_A + 6)
            project(5)
            split_at(U_A + 7)
            project(6)

            def weigh_keys(t):
                w = 128 if t < 2 else NS
                ve.wait_ge(kt_tr, t + 1)
                ve.tensor_tensor(kw[0:w, t, :].rearrange("p (h d) -> p h d", h=H),
                                 bank[6 + t % 2][0:w, :].rearrange("p (h d) -> p h d", h=H),
                                 cols[0:w, t, 32:40].unsqueeze(2).to_broadcast([w, H, DK]), ALU.mult
                                 ).then_inc(kw_done, 1)

            ve.wait_ge(cols_done, 2)
            weigh_keys(0)
            weigh_keys(1)
            split_at(U_A + 8)
            weigh_keys(2)

            def decay(h):
                hp, r = h // 2, slice(64 * (h % 2), 64 * (h % 2) + 64)
                ve.wait_ge(head_s, h + 1)
                for t, (o, i) in enumerate((((0, 256), 0), ((256, 384), 128), ((384, 448), 256))):
                    ins = ve.scalar_tensor_tensor(
                        out=dmat[:, o[0]:o[1]], in0=bank[4][:, i:i + o[1] - o[0]], scalar=cols[:, t, h:h + 1],
                        in1=con[:, C_CAP + o[0]:C_CAP + o[1]], op0=ALU.add, op1=ALU.min)
                ins.then_inc(d_done, 1)
                for half in range(2):
                    ve.tensor_tensor(
                        qm[64 * half:64 * half + 64, h % 2, :].rearrange("p (a x) -> p a x", a=4)[
                            :, :, 8 * half:8 * half + 8],
                        qT[r, hp, TP:T].rearrange("p (a s t) -> p a s t", a=4, s=2)[:, :, half, :],
                        bank[4][r, T:384].rearrange("p (a s t) -> p a s t", a=4, s=2)[:, :, half, :],
                        ALU.mult).then_inc(qm_done, 1)

            def weights(h):
                ve.wait_ge(w_done, h + 1)
                ve.tensor_tensor(pmat[:, 0:448], bank[5][:, 0:448], dmat[:, :], ALU.mult).then_inc(p_done, 1)

            def outputs(h):
                o3 = bank[6][:, 0:3 * (DV + 1)].rearrange("p (t d) -> p t d", t=3)
                ve.wait_ge(head_o, h + 1)
                chain.link(ve.tensor_scalar(den[:, :].unsqueeze(2), o3[:, :, DV:DV + 1], -1.0, None, ALU.mult))
                ve.tensor_tensor(den[:, :].unsqueeze(2), den[:, :].unsqueeze(2),
                                 o3[:, :, DV:DV + 1], ALU.max).then_inc(den_done, 1)
                ve.wait_ge(den_done, h + 1)
                chain.link(ve.tensor_tensor(den[:, :].unsqueeze(2), den[:, :].unsqueeze(2),
                                            cols[:, :, 96 + h:97 + h], ALU.max))
                chain.link(ve.scalar_tensor_tensor(out=den[:, :], in0=den[:, :], scalar=EPS, in1=den[:, :],
                                                   op0=ALU.mult, op1=ALU.mult))
                ve.wait_ge(ssq_h, 3 * h + 3)
                ve.scalar_tensor_tensor(out=var[:, :], in0=ssqh[:, :], scalar=1.0 / DV, in1=den[:, :],
                                        op0=ALU.mult, op1=ALU.add).then_inc(s_in, 1)

            def states(h):
                if h >= 1:
                    ve.wait_ge(cn_out, 16 * h)
                for a in range(4):
                    ins = ve.scalar_tensor_tensor(
                        out=cn[:, a, :], in0=c0[:, h % 2, a, 0:DV], scalar=acb[:, a, h:h + 1],
                        in1=bank[7][:, a * 128:a * 128 + 128], op0=ALU.mult, op1=ALU.add)
                ins.then_inc(cn_done, 1)

            def gated(h):
                ve.wait_ge(ot_tr, h + 1)
                ve.wait_ge(og_done, h + 1)
                ve.scalar_tensor_tensor(out=og[:, h, :], in0=bank[3][:, 0:T],
                                        scalar=par[:, P_HEAD + h:P_HEAD + h + 1], in1=og[:, h, :],
                                        op0=ALU.mult, op1=ALU.mult).then_inc(z_done, 1)

            def z_split(h):
                ve.wait_ge(hh_done, 2 * KT + h + 1)
                ve.tensor_tensor(h_lo[:, h, :], og[:, h, :], h_hi[:, h, :].bitcast(f32), ALU.subtract
                                 ).then_inc(hl_done, 1)

            decay(0)
            weights(0)
            project(7)
            split_at(U_A + 9)
            keep_gate(0)
            gate_half(0)
            for h in range(H):
                outputs(h)
                if h + 1 < H:
                    decay(h + 1)
                    states(h)
                    weights(h + 1)
                    for k, part in HALVES.get(h, ()):
                        split_half(U_A + k, U_A + k, part)
                    keep_gate(h + 1)
                    gated(h)
                    gate_half(h + 1)
                else:
                    states(h)
                    for g in range(H - 1):
                        z_split(g)
                    gated(h)
                    z_split(h)
                    for k, part in HALVES.get(h, ()):
                        split_half(U_A + k, U_A + k, part)
            ve.wait_ge(n_mm, 1)
            chain.link(ve.tensor_copy(al[:, :], bank[5][0:8, 0:8]))
            ve.wait_ge(s_n0, 16)
            chain.link(ve.tensor_tensor(n0[:, :, :], n0[:, :, :],
                                        al[:, :].unsqueeze(2).to_broadcast([NB, H, DK]), ALU.mult))
            ve.tensor_tensor(nn[:, :, :], n0[:, :, :], bank[6][0:8, :].rearrange("p (h d) -> p h d", h=H),
                             ALU.add).then_inc(n_done, 1)
            ve.tensor_copy(npp, bank[4][0:1, :]).then_inc(n_done, 1)
            add_pair(U_OA, P_OA, 0)
            split_at(U_OA + 2)
            add_pair(U_OA, P_OA, 1)
            split_at(U_OA + 3)
            add_pair(U_OA, P_OA, 2)
            split_at(U_OA + 4)

            def after_oa():
                add_pair(U_OA, P_OA, 3)
                for m in range(KT):
                    h_lo_of(m, N_A2, 3 * KT + m + 1)
                split_at(U_FFN[1] + 1)
                rms_of(2)
                ve.wait_ge(s_out, 16 * 3)
                ve.wait_ge(cn_out, 16 * H)
                ve.wait_ge(cp_out_s, 16 * H)

            ffn(1, N_KV, 4 * KT, after_oa)

            def kv_post(k):
                b = 2 * ((P_KV + k) % 2)
                ve.wait_ge(unit_done, U_KV + k + 1)
                if k >= 6:
                    ve.wait_ge(tr_done, 8 + 2 * (k - 5))
                for c in range(2):
                    dst = k_all[:, 2 * k + c, :] if k < 4 else v_st[:, k % 2, c, :]
                    ins = ve.tensor_tensor(dst, bank[b + c][:, 0:T], rms[:, :], ALU.mult)
                ins.then_inc(pair_free, 1)

            add_out(1, KT - 1)
            split_at(U_KV + 1)
            h_lo_of(KT - 1, N_KV, 5 * KT)
            rms_of(3)
            for k in range(1, 8):
                kv_post(k - 1)
                split_at(U_KV + k + 1)

            def after_kv():
                kv_post(7)
                for m in range(KT):
                    h_lo_of(m, N_B0, 5 * KT + m + 1)
                split_at(U_FFN[2] + 1)

            ffn(2, N_B1, 6 * KT, after_kv)

            def q_post(k):
                b = 2 * ((P_Q + k) % 2)
                ve.wait_ge(unit_done, U_Q + k + 1)
                for c in range(2):
                    ins = ve.scalar_tensor_tensor(out=qa[:, 2 * k + c, :], in0=bank[b + c][:, 0:T],
                                                  scalar=128 ** -0.5, in1=rms[:, :],
                                                  op0=ALU.mult, op1=ALU.mult)
                ins.then_inc(pair_free, 1)

            def own(spread):
                return spread[:, :, :].rearrange("p h (b x) -> p h b x", b=NB)[:, :, :, 0:TS]

            add_out(2, KT - 1)
            split_at(U_Q + 1)
            h_lo_of(KT - 1, N_B1, 7 * KT)
            rms_of(4)
            q_post(0)
            split_at(U_Q + 2)
            q_post(1)
            split_at(U_Q + 3)
            q_post(2)
            q_post(3)
            ve.wait_ge(pair_free, P_Q + 4)
            ve.wait_ge(spread_set, 2)
            ve.tensor_copy(own(spread0), qa[:, :, TP:T].rearrange("p h (b t) -> p h b t", b=NB)
                           ).then_inc(qa_sp, 1)

            def prompt_bias(h):
                ve.wait_ge(pr_s, h + 1)
                if h >= 2:
                    ve.wait_ge(pr_t, h - 1)
                ve.scalar_tensor_tensor(out=pp[:, h % 2, :], in0=con[:, C_ND:C_ND + 384], scalar=SLOPE[h],
                                        in1=bank[5][:, 0:384], op0=ALU.mult, op1=ALU.add).then_inc(pr_b, 1)
                ve.wait_ge(pr_b, h + 1)
                for i, c in enumerate((slice(0, 128), slice(128, 384))):
                    ve.tensor_reduce(st[:, h % 2, i:i + 1], pp[:, h % 2, c], AX.X, ALU.max, negate=True
                                     ).then_inc(pr_m, 1)

            def prompt_probs(h):
                ve.wait_ge(pr_e, 2 * h + 2)
                chain.link(ve.reciprocal(st[:, h % 2, 4:6], st[:, h % 2, 2:4]))
                for i, c in enumerate((slice(0, 128), slice(128, 384))):
                    ins = ve.tensor_scalar(pp[:, h % 2, c], pp[:, h % 2, c], st[:, h % 2, 4 + i:5 + i], None,
                                           ALU.mult)
                ins.then_inc(pr_p, 1)

            def prompt_lo(h):
                ve.wait_ge(pr_hi, h + 1)
                ve.tensor_tensor(h_lo[:, h, 0:TP], bank[7][:, 0:TP], h_hi[:, h, 0:TP].bitcast(f32),
                                 ALU.subtract).then_inc(pr_lo, 1)

            for b in range(NB):
                prompt_bias(b)
                prompt_probs(b)
                if b >= 1:
                    prompt_lo(b - 1)

            ve.wait_ge(new_s, 1)
            ve.wait_ge(kv_used, NB)
            for h in range(H):
                ve.scalar_tensor_tensor(out=ss[:, h, 0:PAST], in0=con[0:NS, C_NDS:C_NDS + PAST],
                                        scalar=SLOPE[h],
                                        in1=bank[h // 2][0:NS, (h % 2) * PAST:(h % 2) * PAST + PAST],
                                        op0=ALU.mult, op1=ALU.add)
                chain.link(ve.scalar_tensor_tensor(
                    out=ss[:, h, PAST:PAST + NS], in0=con[0:NS, C_NDS + PAST:C_NDS + PAST + NS],
                    scalar=SLOPE[h], in1=bank[4][0:NS, h * NS:h * NS + NS], op0=ALU.mult, op1=ALU.add))
                ve.tensor_reduce(sst[:, 0, h:h + 1], ss[:, h, :], AX.X, ALU.max, negate=True).then_inc(sm_m, 1)
            for h in range(H):
                ve.wait_ge(sm_e, h + 1)
                chain.link(ve.reciprocal(sst[:, 2, h:h + 1], sst[:, 1, h:h + 1]))
                ve.tensor_scalar(ss[:, h, :], ss[:, h, :], sst[:, 2, h:h + 1], None, ALU.mult).then_inc(sm_p, 1)
            for g, spread in enumerate((spread0, spread1)):
                ve.wait_ge(sm_t, g + 1)
                ve.tensor_copy(own(spread), bank[g][:, :].rearrange("p (h b t) -> p h b t", h=H, b=NB)
                               ).then_inc(sm_tc, 1)
            prompt_lo(NB - 1)
            split_at(U_OB)
            split_at(U_OB + 1)
            ve.wait_ge(sm_hi, 1)
            ve.tensor_tensor(h_lo[:, :, TP:T], bank[0][:, :].rearrange("p (h t) -> p h t", h=H),
                             h_hi[:, :, TP:T].bitcast(f32), ALU.subtract).then_inc(sm_lo, 1)
            for k in range(3):
                add_pair(U_OB, P_OB, k)
                split_at(U_OB + 2 + k)

            def after_ob():
                add_pair(U_OB, P_OB, 3)
                for m in range(KT):
                    h_lo_of(m, N_B2, 7 * KT + m + 1)
                split_at(U_FFN[3] + 1)
                rms_of(5)

            ffn(3, None, 0, after_ob)
            add_out(3, KT - 1)
            rms_of(6)
            for m in range(KT):
                ve.scalar_tensor_tensor(out=x[:, m, :], in0=x[:, m, :],
                                        scalar=par[:, P_G + KT * N_FIN + m:P_G + KT * N_FIN + m + 1],
                                        in1=rms[:, :], op0=ALU.mult, op1=ALU.mult).then_inc(y_done, 1)

        @block.gpsimd
        def _(gp):
            def add_squares(j):
                for m in range(KT):
                    c = KT * j + m
                    gp.wait_ge(sq_done, c + 1)
                    if m == 0:
                        if j >= 1:
                            gp.wait_ge(ssq_done, j)
                        gp.tensor_copy(sqsum[:, :], sq[:, m % 2, :]).then_inc(sum_done, 1)
                    else:
                        gp.wait_ge(sum_done, c)
                        gp.tensor_tensor(sqsum[:, :], sqsum[:, :], sq[:, m % 2, :], ALU.add).then_inc(sum_done, 1)

            gp.memset(epsc[:, :], EPS).then_inc(s_set, 1)
            gp.memset(mhalf[:, :], -0.5).then_inc(s_set, 1)
            gp.memset(v_tok[:, :, :, DV:DV + 1], 1.0).then_inc(s_set, 1)
            gp.memset(v_tok[:, 2, :, 0:DV], 0.0).then_inc(s_set, 1)
            gp.wait_ge(s_set, 4)
            add_squares(0)
            add_squares(1)
            gp.wait_ge(unit_done, U_A)
            gp.memset(rows[:, :], 0.0).then_inc(zero_done, 1)
            gp.memset(kT[:, :, T:384], 0.0).then_inc(zero_done, 1)
            gp.memset(cols[:, 2, :], 1.0).then_inc(zero_done, 1)
            gp.memset(pmat[:, 448:512], 0.0)
            gp.memset(qm[:, :, :], 0.0).then_inc(zero_done, 1)
            gp.dma_start(n0[:, :, :].rearrange("b h d -> b (h d)"), n0_in).then_inc(s_n0, 16)
            for h in range(2):
                gp.dma_start(c0[:, h, :, :], c0_in[h]).then_inc(c0_load[h], 16)
            gp.wait_ge(mo_done, 2)
            gp.dma_start(m_out, mo[:, :]).then_inc(s_out, 16)

            def keys_of(h):
                if h >= 2:
                    gp.wait_ge(head_o, h - 1)
                gp.tensor_tensor(kwm[:, h % 2, :, :],
                                 kw[0:NS, 2, h * DK:h * DK + DK].unsqueeze(1).to_broadcast([NS, NB, DK]),
                                 con[0:NS, C_BM:C_BM + NB].unsqueeze(2).to_broadcast([NS, NB, DK]), ALU.mult
                                 ).then_inc(kwm_done, 1)

            gp.wait_ge(kw_done, 3)
            keys_of(0)
            keys_of(1)
            for h in range(H):
                gp.wait_ge(s_in, h + 1)
                gp.tensor_tensor(scl[:, :], var[:, :], mhalf[:, :], ALU.pow).then_inc(s_pow, 1)
                gp.wait_ge(cp_done, h + 1)
                gp.dma_start(cp_out[h], cpn[:, :]).then_inc(cp_out_s, 16)
                gp.wait_ge(cn_done, h + 1)
                gp.dma_start(cs_out[h], cn[:, :, :]).then_inc(cn_out, 16)
                if h + 2 < H:
                    gp.dma_start(c0[:, h % 2, :, :], c0_in[h + 2]).then_inc(c0_load[h % 2], 16)
                    keys_of(h + 2)
            gp.wait_ge(n_done, 2)
            gp.dma_start(ns_out, nn[:, :, :].rearrange("b h d -> b (h d)")).then_inc(s_out, 16)
            gp.dma_start(np_out, npp).then_inc(s_out, 16)
            add_squares(2)
            add_squares(3)
            gp.wait_ge(tr_free, 16)
            gp.dma_start(k_out, k_all[:, :, :]).then_inc(s_out, 16)
            gp.dma_start(v_out, v_tok[:, :, :, 0:DV]).then_inc(s_out, 16)
            add_squares(4)
            gp.wait_ge(unit_done, U_Q)
            gp.memset(spread0[:, :, :], 0.0).then_inc(spread_set, 1)
            gp.memset(spread1[:, :, :], 0.0).then_inc(spread_set, 1)
            add_squares(5)
            add_squares(6)


def _constants():
    import numpy as np
    con = np.zeros((128, C_COLS), np.float32)
    p = np.arange(128)[:, None]
    con[:, C_ID:C_ID + 128] = np.eye(128)
    con[:, C_ONE:C_ONE + 128] = 1.0
    s, t = p, np.arange(256)[None, :]
    con[:, C_CAP:C_CAP + 256] = np.where(s <= t, 0.0, -BIG)
    con[:, C_CAP + 256:C_CAP + 384] = np.where(s <= t[:, :128], 0.0, -BIG)
    ts = np.arange(NS)[None, :]
    con[:, C_CAP + 384:C_CAP + 448] = np.where((p < NS) & (p // TS == ts // TS) & (p <= ts), 0.0, -BIG)
    masked = -1e30
    con[:, C_ND:C_ND + 128] = np.where(t[:, :128] <= p, t[:, :128] - p, masked)
    con[:, C_ND + 128:C_ND + 384] = np.where(t <= 128 + p, t - 128 - p, masked)
    con[:, C_NDS:C_NDS + 256] = t - (PAST + p % TS)
    con[:, C_NDS + 256:C_NDS + 320] = np.where((p // TS == ts // TS) & (ts <= p), ts - p, masked)
    con[:, C_BM:C_BM + 8] = p // TS == np.arange(8)[None, :]
    con[:, C_LAST:C_LAST + 8] = p == np.arange(8)[None, :] * TS + TS - 1
    row = np.zeros((8, R_COLS), np.float32)
    row[:, R_SEL:R_SEL + 1024] = np.repeat(np.eye(8), 128, axis=1)
    row[:, R_HALF:R_HALF + 64] = 1.0
    row[:, R_HALF + 192:R_HALF + 256] = 1.0
    starts = np.zeros(T, bool)
    starts[0] = True
    starts[TP::TS] = True
    row[:, R_MUL:R_MUL + T] = np.where(starts, 0.0, 1.0)
    row[:, R_NEG:R_NEG + T] = np.where(starts, -BIG, 0.0)
    row[:, R_DEL:R_DEL + 8] = np.eye(8)
    return con, row


def _pair_units(w, first, second):
    import numpy as np
    a = w.reshape(KT, 128, -1)
    out = np.empty((len(first), 128, 2, KT, 128), w.dtype)
    for u, (i, j) in enumerate(zip(first, second)):
        out[u, :, 0] = a[:, :, i:i + 128].transpose(1, 0, 2)
        out[u, :, 1] = a[:, :, j:j + 128].transpose(1, 0, 2)
    return out.reshape(len(first), 128, PAIR)


def _plain_units(w):
    n = w.shape[1] // 256
    return _pair_units(w, [256 * u for u in range(n)], [256 * u + 128 for u in range(n)])


def kernel(**inputs):
    import numpy as np
    import concourse.bacc as bacc
    from concourse import mybir as mb
    from concourse.bass_utils import run_bass_kernel_spmd as run

    a = {k: np.asarray(v) for k, v in inputs.items()}
    w_ffn_in = a["w_ffn_in"].reshape(4, D, 2 * FF)
    w_ffn_out = a["w_ffn_out"].reshape(4, FF, D)
    HK, HV = H * DK, H * DV
    w_in_a = a["w_in_a"][0]
    a_first = [*range(HK, 2 * HK + HV, 256), *range(0, HK, 256), *range(2 * HK + HV, 2 * HK + 2 * HV, 256)]
    gate_w = np.zeros((128, KT, 40), np.float32)
    g = w_in_a[:, 2 * HK + 2 * HV:].reshape(KT, 128, 2 * H).transpose(1, 0, 2)
    gate_w[:, :, 0:8], gate_w[:, :, 32:40] = g[:, :, 0:8], g[:, :, 8:16]
    par = np.zeros((128, P_COLS), np.float32)
    gains = [a["g_norm"][0, 0], a["g_norm"][0, 1], a["g_norm"][0, 2], a["g_kv"],
             a["g_norm"][1, 0], a["g_norm"][1, 1], a["g_norm"][1, 2], a["g_final"]]
    for i, v in enumerate(gains):
        par[:, P_G + KT * i:P_G + KT * i + KT] = v.reshape(KT, 128).T
    par[:, P_HEAD:P_HEAD + H] = a["g_head_a"][0].reshape(H, DV).T
    par[0:8, P_BI] = a["b_gate_a"][0, 0:8]
    par[32:40, P_BF] = a["b_gate_a"][0, 8:16]
    con, row = _constants()
    row[:, R_M0 + TP:R_M0 + T] = np.repeat(a["state_m"][0].T, TS, axis=1)
    xs = np.concatenate([a["x_prompt"].reshape(TP, D), a["x_sample"].reshape(NS, D)])
    c0 = np.empty((H, 2, DK, 4, DV + 1), np.float32)
    c0[..., 0:DV] = a["state_c"][0].reshape(4, 2, H, DK, DV).transpose(2, 1, 3, 0, 4)
    c0[..., DV] = a["state_n"][0].reshape(4, 2, H, DK).transpose(2, 1, 3, 0)
    n_pool = a["cache_k"].shape[0]
    arrays = {
        "w_in": np.stack([_pair_units(w, [128 * i for i in range(FK)], [FF + 128 * i for i in range(FK)])
                          for w in w_ffn_in]),
        "w_out": np.ascontiguousarray(w_ffn_out.reshape(4, 2, HALF, 128, KT, 128).transpose(0, 4, 1, 3, 2, 5)
                                      ).reshape(4, 2 * KT, 128, OUTU),
        "w_a": _pair_units(w_in_a, a_first, [c + 128 for c in a_first]),
        "w_oa": _plain_units(a["w_out_a"][0]),
        "w_kv": _plain_units(a["w_kv"]),
        "w_q": _plain_units(a["w_q_b"][0]),
        "w_ob": _plain_units(a["w_out_b"][0]),
        "w_gate": gate_w,
        "x_in": np.ascontiguousarray(xs.reshape(T, KT, 128).transpose(2, 1, 0)),
        "par_in": par, "con_in": con, "row_in": row,
        "c0_in": c0.reshape(H, 128, 4, DV + 1),
        "n0_in": np.ascontiguousarray(a["state_n"][0].reshape(NB, H * DK)),
        "kc_in": np.ascontiguousarray(a["cache_k"].transpose(0, 3, 2, 1)).reshape(n_pool, 128, H * PAGE),
        "vc_in": np.ascontiguousarray(a["cache_v"]).reshape(n_pool, 128, H * 128),
        "pt_in": np.ascontiguousarray(a["page_table"].reshape(1, NB * NPG)),
    }
    outs = {"y_out": (128, KT, T), "k_out": (128, H, T), "v_out": (128, 3, H, DV), "cp_out": (H, DK, DV),
            "cs_out": (H, 128, 4, DV), "np_out": (1, H * DK), "ns_out": (NB, H * DK), "m_out": (8, 1 + NB)}
    nc = bacc.Bacc("TRN2", target_bir_lowering=False, num_devices=1)
    args = {n: nc.dram_tensor(n, v.shape, mb.dt.from_np(v.dtype), kind="ExternalInput").ap()
            for n, v in arrays.items()}
    args |= {n: nc.dram_tensor(n, s, mb.dt.float32, kind="ExternalOutput").ap() for n, s in outs.items()}
    trunk_program(nc, **args)
    r = run(nc, [arrays], core_ids=[0]).results[0]
    y = r["y_out"].transpose(2, 1, 0).reshape(T, D)
    k = r["k_out"].transpose(2, 1, 0)
    v = r["v_out"].transpose(1, 0, 2, 3).reshape(3 * 128, H, DV)
    cs = r["cs_out"].reshape(H, 2, DK, 4, DV).transpose(3, 1, 0, 2, 4).reshape(1, NB, H, DK, DV)
    out = (y[:TP].reshape(1, TP, D), y[TP:].reshape(NB, TS, D),
           r["cp_out"].reshape(1, 1, H, DK, DV), r["np_out"].reshape(1, 1, H, DK),
           r["m_out"][:, 0].reshape(1, 1, H), k[:TP].reshape(1, TP, H, 128), v[:TP].reshape(1, TP, H, 128),
           cs, r["ns_out"].reshape(1, NB, H, DK), r["m_out"][:, 1:].T.reshape(1, NB, H),
           k[TP:].reshape(NB, TS, H, 128), v[TP:T].reshape(NB, TS, H, 128))
    return tuple(np.ascontiguousarray(o) for o in out)
```

```python
from contextlib import ExitStack

import concourse.bass as bass
from concourse import mybir

D = 1024
KT = D // 128
TP, NB, TS = 256, 8, 8
NS = NB * TS
T = TP + NS
FF = 2816
FK = FF // 128
HALF = FK // 2
H = 8
DK, DV = 64, 128
HP = H // 2
PAST, PAGE = 256, 128
NPG = PAST // PAGE
EPS = 1e-6
BIG = 3e38
PAIR = 2 * KT * 128
OUTU = HALF * 128
RAW = 4
QKV_UNITS, O_UNITS = 8, 4
C_ID, C_ONE, C_CAP, C_ND, C_NDS, C_BM, C_LAST = 0, 128, 256, 704, 1088, 1408, 1416
C_COLS = 1424
R_SEL, R_HALF, R_MUL, R_NEG, R_DEL, R_M0 = 0, 1024, 1280, 1600, 1920, 1928
R_COLS = 2248
P_G, P_HEAD, P_BI, P_BF = 0, 64, 72, 73
P_COLS = 74
N_A0, N_A1, N_A2, N_KV, N_B0, N_B1, N_B2, N_FIN = range(8)


def slopes():
    return [2.0 ** (-8.0 * (h + 1) / H) for h in range(H)]


class Chain:

    def __init__(self, eng, sem):
        self.eng, self.sem, self.n = eng, sem, 0

    def link(self, ins):
        self.n += 1
        ins.then_inc(self.sem, 1)
        self.eng.wait_ge(self.sem, self.n)


def trunk_program(nc, w_in, w_out, w_a, w_oa, w_kv, w_q, w_ob, w_gate, x_in, par_in, con_in, row_in,
                  c0_in, n0_in, kc_in, vc_in, pt_in,
                  y_out, k_out, v_out, cp_out, cs_out, np_out, ns_out, m_out):
    f32, f32r, i32 = mybir.dt.float32, mybir.dt.float32r, mybir.dt.int32
    ALU, ACT, AX = mybir.AluOpType, mybir.ActivationFunctionType, mybir.AxisListType
    SLOPE = slopes()
    ctx = ExitStack()
    with ctx:
        def sb(name, shape, dt=f32, where=ctx):
            return where.enter_context(nc.sbuf_tensor(name, shape, dt))

        def sem(name):
            return ctx.enter_context(nc.semaphore(name))

        raw = sb("raw", [128, RAW, PAIR])
        w_hi = sb("w_hi", [128, 2, PAIR], f32r)
        w_lo = sb("w_lo", [128, 2, PAIR], f32r)
        x = sb("x", [128, KT, T])
        h_hi = sb("h_hi", [128, KT, T], f32r)
        h_lo = sb("h_lo", [128, KT, T], f32r)
        rms = sb("rms", [128, T])
        root = sb("root", [128, T])
        sqsum = sb("sqsum", [128, T])
        sq = sb("sq", [128, 2, T])
        work = sb("work", [128, 10 * T])
        gate, up, act = (work[:, 2 * T * i:2 * T * i + 2 * T].rearrange("p (s t) -> p s t", s=2) for i in range(3))
        v_st = work[:, 6 * T:10 * T].rearrange("p (s c t) -> p s c t", s=2, c=2)
        pp = work[:, 0:768].rearrange("p (s k) -> p s k", s=2)
        pt = work[:, 768:1536].rearrange("p (s k) -> p s k", s=2)
        pn = work[0:NS, 1536:2048].rearrange("p (h t) -> p h t", h=H)
        v_tok = sb("v_tok", [128, 3, H, DV + 1])
        con = sb("con", [128, C_COLS])
        row = sb("row", [8, R_COLS])
        par = sb("par", [128, P_COLS])
        wg = sb("wg", [128, KT, 40])
        epsc = sb("epsc", [128, 1])
        pages = sb("pages", [1, NB * NPG], i32)
        mhalf = sb("mhalf", [128, 3])

        with ExitStack() as ov:
            with ExitStack() as own:
                qT = sb("qT", [128, HP, T], f32, own)
                kT = sb("kT", [128, HP, 384], f32, own)
                og = sb("og", [128, H, T], f32, own)
                kw = sb("kw", [128, 3, H * DK], f32, own)
                kwm = sb("kwm", [NS, 2, NB, DK], f32, own)
                rows = sb("rows", [128, T], f32, own)
                cols = sb("cols", [128, 3, 128], f32, own)
                g40 = sb("g40", [40, T], f32, own)
                fz = sb("fz", [8, T], f32, own)
                fa = sb("fa", [8, T], f32, own)
                cb = sb("cb", [8, T], f32, own)
                cm = sb("cm", [8, T], f32, own)
                neg = sb("neg", [8, 384], f32, own)
                mt = sb("mt", [8, T], f32, own)
                tmp = sb("tmp", [8, T], f32, own)
                mo = sb("mo", [8, 1 + NB], f32, own)
                dmat = sb("dmat", [128, 448], f32, own)
                pmat = sb("pmat", [128, 512], f32, own)
                qm = sb("qm", [128, 2, 4 * (NS + 2 * TS)], f32, own)
                c0 = sb("c0", [128, 2, 4, DV + 1], f32, own)
                cn = sb("cn", [128, 4, DV], f32, own)
                cpn = sb("cpn", [DK, DV], f32, own)
                ot = sb("ot", [128, 3, DV], f32, own)
                junk = sb("junk", [128, 3, DV], f32, own)
                ssqh, den, var, scl = (sb(n, [128, 3], f32, own) for n in ("ssqh", "den", "var", "scl"))
                ac_rhs = sb("ac_rhs", [8, 2, 4, H], f32, own)
                acb = sb("acb", [128, 4, H], f32, own)
                n0 = sb("n0", [NB, H, DK], f32, own)
                nn = sb("nn", [NB, H, DK], f32, own)
                al = sb("al", [NB, H], f32, own)
            k_all = sb("k_all", [128, H, T], f32, ov)
            with ExitStack() as own:
                f_hi = sb("f_hi", [128, FK, T], f32r, own)
                f_lo = sb("f_lo", [128, FK, T], f32r, own)
            with ExitStack() as own:
                qa = sb("qa", [128, H, T], f32, own)
                spread0 = sb("spread0", [128, H, NB * (NS + TS)], f32, own)
                spread1 = sb("spread1", [128, H, NB * (NS + TS)], f32, own)
                ss = sb("ss", [NS, H, PAST + NS], f32, own)
                st = sb("st", [128, 2, 6], f32, own)
                sst = sb("sst", [NS, 3, H], f32, own)

        npp = pmat[0:1, :]
        o_rows = qa[0:NS, :, :].rearrange("p h t -> p (h t)")[:, 0:H * DV]
        ident, ones = con[:, C_ID:C_ID + 128], con[:, C_ONE:C_ONE + 128]
        sel = row[:, R_SEL:R_SEL + 1024].rearrange("k (h p) -> k h p", h=H)
        bank = [ctx.enter_context(nc.psum_tensor(f"bank{i}", [128, 512], f32)) for i in range(8)]

        s_par = sem("parameters_loaded")
        s_con = sem("constants_loaded")
        s_x = [sem(f"x_loaded{m}") for m in range(KT)]
        s_n0 = sem("state_n_loaded")
        s_pg = sem("page_table_loaded")
        s_set = sem("small_constants_set")
        loaded = [sem(f"raw_loaded{i}") for i in range(RAW)]
        hi_done = sem("weight_hi_done")
        lo_done = sem("weight_lo_done")
        unit_done = sem("unit_multiplied")
        kv_used = sem("cache_unit_used")
        pair_free = sem("pair_banks_evacuated")
        gate_ready = sem("gate_scaled")
        silu_ready = sem("silu_done")
        hid_ready = sem("hidden_done")
        hid_hi = sem("hidden_hi_done")
        hid_lo = sem("hidden_lo_done")
        x_ready = sem("x_chunk_ready")
        hh_done = sem("h_hi_done")
        hl_done = sem("h_lo_done")
        sq_done = sem("squares_done")
        sum_done = sem("square_sum_done")
        ssq_done = sem("square_total_done")
        root_done = sem("root_done")
        rms_done = sem("rms_done")
        s_dve = sem("vector_steps")
        s_act = sem("scalar_steps")
        s_out = sem("outputs_stored")
        s_y = sem("y_stored")
        y_done = sem("y_chunk_done")
        mo_done = sem("last_m_gathered")
        spread_set = sem("spread_zeros_set")
        sm_tn = sem("sample_new_probs_copied")
        cp_out_s = sem("prompt_state_stored")
        gates_mm = sem("gates_multiplied")
        wgg_done = sem("gate_weights_scaled")
        abs_done = sem("gate_abs_done")
        ln_done = sem("gate_log_done")
        dm_done = sem("m0_minus_m_done")
        mt_done = sem("m_rows_done")
        aw_done = sem("key_weight_rows_done")
        rows_a = sem("rows_by_vector_done")
        rows_b = sem("rows_by_scalar_done")
        rows_t = sem("rows_transposed")
        cols_done = sem("columns_done")
        ac_done = sem("carry_factors_done")
        acb_mm = sem("carry_factors_spread")
        o_even = sem("output_gate_even_chunk_multiplied")
        o_kept = sem("output_gate_chunk_kept")
        tanh_done = sem("output_gate_tanh_done")
        og_done = sem("output_gate_done")
        tr_done = sem("transposes_done")
        tr_free = sem("transposes_evacuated")
        kt_tr = sem("keys_transposed")
        kw_done = sem("weighted_keys_done")
        zero_done = sem("zeros_set")
        head_s = sem("head_scores_done")
        d_done = sem("head_decay_done")
        w_done = sem("head_weights_done")
        p_done = sem("head_products_done")
        qm_done = sem("head_queries_spread")
        kwm_done = sem("head_keys_spread")
        c0_load = [sem("state_c_loaded0"), sem("state_c_loaded1")]
        head_o = sem("head_outputs_done")
        cp_done = sem("prompt_state_copied")
        cn_done = sem("sample_state_done")
        cn_out = sem("sample_state_stored")
        den_done = sem("head_denominators_read")
        ssq_h = sem("head_squares_done")
        s_in = sem("head_scale_in_done")
        s_pow = sem("head_scale_done")
        ot_done = sem("head_scaled")
        ot_tr = sem("head_transposed")
        z_done = sem("head_gated")
        n_mm = sem("n_multiplied")
        n_done = sem("n_done")
        qa_sp = sem("queries_spread")
        new_s = sem("new_scores_done")
        pr_s = sem("prompt_scores_done")
        pr_b = sem("prompt_scores_biased")
        pr_m = sem("prompt_max_done")
        pr_e = sem("prompt_exp_done")
        pr_p = sem("prompt_probs_done")
        pr_t = sem("prompt_probs_transposed")
        pr_tc = sem("prompt_probs_copied")
        pr_o = sem("prompt_outputs_done")
        pr_hi = sem("prompt_outputs_hi")
        pr_lo = sem("prompt_outputs_lo")
        sm_m = sem("sample_max_done")
        sm_e = sem("sample_exp_done")
        sm_r = sem("sample_sums_inverted")
        sm_t = sem("sample_probs_transposed")
        sm_tc = sem("sample_probs_spread")
        sm_oc = sem("sample_outputs_copied")
        sm_ot = sem("sample_outputs_transposed")
        sm_hi = sem("sample_outputs_hi")
        sm_lo = sem("sample_outputs_lo")

        FFN_UNITS = FK + 2 * KT
        U_FFN = [0, 0, 0, 0]
        at = 0
        U_FFN[0] = at; at += FFN_UNITS
        U_A = at; at += QKV_UNITS + O_UNITS
        U_OA = at; at += 4
        U_FFN[1] = at; at += FFN_UNITS
        U_KV = at; at += 8
        U_FFN[2] = at; at += FFN_UNITS
        U_Q = at; at += 4
        U_OB = at; at += 4
        U_FFN[3] = at; at += FFN_UNITS
        U_END = at
        CACHE = 2 * NB

        P_A = FK
        P_OA = P_A + QKV_UNITS
        P_KV = P_OA + FK
        P_Q = P_KV + 8 + FK
        P_OB = P_Q + 4
        P_FFN = [0, P_OA, P_KV + 8, P_OB]

        HALVES = {1: ((10, 0),), 2: ((10, 1),), 3: ((11, 0),), 4: ((11, 1),), 5: ((12, 0),), 6: ((12, 1),),
                  7: ((13, 0), (13, 1))}
        XB = [0, 2 * KT, 3 * KT, 5 * KT]

        block = ctx.enter_context(nc.Block())

        def loads_after(r):
            return sum(64 if U_OB <= q < U_OB + CACHE else 16 for q in range(r % RAW, r + 1, RAW))

        def raw_of(n):
            return n + (CACHE if n >= U_OB else 0)

        def width(n):
            return OUTU if any(f + FK <= n < f + FFN_UNITS for f in U_FFN) else PAIR

        @block.sync
        def _(sp):
            def load(r, src, w):
                before = r - RAW
                if 0 <= before < U_OB:
                    sp.wait_ge(lo_done, before + 1)
                elif U_OB <= before < U_OB + CACHE:
                    sp.wait_ge(kv_used, before - U_OB + 1)
                elif before >= 0:
                    sp.wait_ge(lo_done, before - CACHE + 1)
                sp.dma_start(raw[:, r % RAW, 0:w], src).then_inc(loaded[r % RAW], 16)

            def ffn(f):
                base = raw_of(U_FFN[f])
                for k in range(RAW):
                    load(base + k, w_in[f, k], PAIR)
                    if f == 0 and k == 0:
                        for m in range(KT):
                            sp.dma_start(x[:, m, :], x_in[:, m, :]).then_inc(s_x[m], 16)
                    if f == 0 and k == 1:
                        sp.dma_start(con[:, :], con_in).then_inc(s_con, 16)
                        sp.dma_start(row[:, :], row_in).then_inc(s_con, 16)
                        sp.dma_start(wg[:, :, :], w_gate).then_inc(s_con, 16)
                        sp.dma_start(pages[:, :], pt_in).then_inc(s_pg, 16)
                with sp.Fori(0, (FK - RAW) // RAW) as i:
                    for j in range(RAW):
                        sp.wait_ge(lo_done, i * RAW + (U_FFN[f] + j + 1))
                        sp.dma_start(raw[:, (base + j) % RAW, 0:PAIR],
                                     w_in[f, bass.ds(i * RAW + (RAW + j), 1)].rearrange("a p c -> p (a c)")
                                     ).then_inc(loaded[(base + j) % RAW], 16)
                for k in range(FK - FK % RAW, FK):
                    load(base + k, w_in[f, k], PAIR)
                for k in range(2 * KT):
                    load(base + FK + k, w_out[f, k], OUTU)

            sp.dma_start(par[:, :], par_in).then_inc(s_par, 16)
            ffn(0)
            for k in range(QKV_UNITS + O_UNITS):
                load(U_A + k, w_a[k], PAIR)
            for k in range(4):
                load(U_OA + k, w_oa[k], PAIR)
            ffn(1)
            for k in range(8):
                load(U_KV + k, w_kv[k], PAIR)
            ffn(2)
            for k in range(4):
                load(U_Q + k, w_q[k], PAIR)
            sp.wait_ge(s_pg, 16)
            for i in range(CACHE):
                r = U_OB + i
                src = kc_in if i < NB else vc_in
                heads = slice(512 * (i // 4 % 2), 512 * (i // 4 % 2) + 512)
                if r - RAW < U_OB:
                    sp.wait_ge(lo_done, r - RAW + 1)
                else:
                    sp.wait_ge(kv_used, r - RAW - U_OB + 1)
                for j in range(2 * NPG):
                    at = 2 * NPG * (i % 4) + j
                    page = sp.value_load(pages[0:1, at:at + 1], min_val=0, max_val=kc_in.shape[0] - 1)
                    sp.dma_start(raw[:, r % RAW, j * 512:j * 512 + 512],
                                 src[bass.ds(page, 1), :, heads].rearrange("a p c -> p (a c)")
                                 ).then_inc(loaded[r % RAW], 16)
            for k in range(4):
                load(U_OB + CACHE + k, w_ob[k], PAIR)
            ffn(3)
            for m in range(KT):
                sp.wait_ge(y_done, m + 1)
                sp.dma_start(y_out[:, m, :], x[:, m, :]).then_inc(s_y, 16)
            sp.wait_ge(s_y, 16 * KT)
            sp.wait_ge(cn_out, 16 * H)
            sp.wait_ge(cp_out_s, 16 * H)
            sp.wait_ge(s_out, 16 * 5)

        @block.tensor
        def _(pe):
            def passes(out, wh, wl, mh, ml, first, last):
                pe.matmul(out, wh, mh, start=first, stop=False)
                pe.matmul(out, wh, ml, start=False, stop=False)
                return pe.matmul(out, wl, mh, start=False, stop=last)

            def chunk(out, s, c):
                for kt in range(KT):
                    mm = chunk_part(out, s, c, kt)
                return mm

            def chunk_part(out, s, c, kt):
                w = (c * KT + kt) * 128
                return passes(out, w_hi[:, s, w:w + 128], w_lo[:, s, w:w + 128],
                              h_hi[:, kt, :], h_lo[:, kt, :], kt == 0, kt == KT - 1)

            def split_at_kt(count):
                return lambda kt: pe.wait_ge(hl_done, count + kt + 1)

            def pair_unit(n, p, n_at, p_at, h_wait=None, between=None, added=None):
                pe.wait_ge(lo_done, n + 1)
                if added:
                    pe.wait_ge(x_ready, added)
                elif p_at >= 2:
                    pe.wait_ge(pair_free, p - 1)
                b = 2 * (p_at % 2)
                if h_wait is None:
                    chunk(bank[b][:, 0:T], n_at % 2, 0)
                    chunk(bank[b + 1][:, 0:T], n_at % 2, 1).then_inc(unit_done, 1)
                else:
                    for kt in range(KT):
                        if kt == KT - 1 and between:
                            between()
                        h_wait(kt)
                        for c in range(2):
                            mm = chunk_part(bank[b + c][:, 0:T], n_at % 2, c, kt)
                    mm.then_inc(unit_done, 1)

            def units(u, p, first, end, **kw0):
                for k in range(first, end):
                    pair_unit(u + k, p + k, u + k, p + k, **(kw0 if k == first else {}))

            def units_to_x(u, p, xbase, first, end, h_wait=None):
                for k in range(first, end):
                    pair_unit(u + k, p + k, u + k, p + k, h_wait if k == 0 else None,
                              added=xbase + 2 * k - 2 if k >= 2 else None)

            def total(j):
                pe.wait_ge(sum_done, KT * (j + 1))
                if j == 0:
                    pe.wait_ge(s_con, 48)
                else:
                    pe.wait_ge(root_done, j)
                pe.matmul(bank[6][:, 0:T], ones, sqsum[:, :], start=True, stop=True).then_inc(ssq_done, 1)

            def ffn(f, h_wait, between, behind=None):
                u, p = U_FFN[f], P_FFN[f]
                pair_unit(u, p, u, p, h_wait, between)
                if behind:
                    behind()
                units(u, p, 1, 3)
                with pe.Fori(0, (FK - 4) // 2) as i:
                    for j in (3, 4):
                        pair_unit(i * 2 + (u + j), i * 2 + (p + j), u + j, p + j)
                pair_unit(u + FK - 1, p + FK - 1, u + FK - 1, p + FK - 1)

                def out_chunk(m, m_at, wait_hidden):
                    out = bank[4 + m_at % 2][:, 0:T]
                    if m_at >= 2:
                        pe.wait_ge(x_ready, m + (XB[f] - 1))
                    for part in range(2):
                        pe.wait_ge(lo_done, m * 2 + (u + FK + part + 1))
                        s = (u + FK + part) % 2
                        for kt in range(HALF):
                            g = part * HALF + kt
                            if wait_hidden:
                                pe.wait_ge(hid_lo, FK * f + g + 1)
                            mm = passes(out, w_hi[:, s, kt * 128:kt * 128 + 128],
                                        w_lo[:, s, kt * 128:kt * 128 + 128],
                                        f_hi[:, g, :], f_lo[:, g, :], g == 0, g == FK - 1)
                        mm.then_inc(unit_done, 1)

                out_chunk(0, 0, True)
                out_chunk(1, 1, False)
                with pe.Fori(0, (KT - 2) // 2) as i:
                    for j in (2, 3):
                        out_chunk(i * 2 + j, j, False)

            groups = [0]

            def turn_values(p, v_unit):
                pe.wait_ge(pair_free, p + 1)
                for c in range(2):
                    g = groups[0]
                    groups[0] += 1
                    if g >= 2:
                        pe.wait_ge(tr_free, g - 1)
                    for t in range(3):
                        w = 128 if t < 2 else NS
                        mm = pe.transpose(bank[4 + g % 2][0:w, t * 128:t * 128 + 128],
                                          v_st[:, v_unit % 2, c, t * 128:t * 128 + w], ident)
                    mm.then_inc(tr_done, 1)

            ffn(0, split_at_kt(0), lambda: total(0))

            def gates():
                total(1)
                pe.wait_ge(wgg_done, KT)
                for kt in range(KT):
                    mm = pe.matmul(bank[7][0:40, 0:T], wg[:, kt, :], x[:, kt, :],
                                   start=(kt == 0), stop=(kt == KT - 1))
                mm.then_inc(gates_mm, 1)

            def turn_rows():
                pe.wait_ge(rows_a, 1)
                pe.wait_ge(rows_b, 4)
                for t in range(3):
                    w = 128 if t < 2 else NS
                    mm = pe.transpose(bank[6][0:w, t * 128:t * 128 + 128], rows[:, t * 128:t * 128 + w], ident)
                mm.then_inc(rows_t, 1)
                pe.wait_ge(ac_done, 2)
                for half in range(2):
                    mm = pe.matmul(bank[7][:, 0:32], row[:, R_HALF + 128 * half:R_HALF + 128 * half + 128],
                                   ac_rhs[:, half, :, :].rearrange("k a h -> k (a h)"),
                                   start=(half == 0), stop=(half == 1))
                mm.then_inc(acb_mm, 1)

            def turn_keys(t):
                if t < 2:
                    pe.wait_ge(cols_done, 3)
                else:
                    pe.wait_ge(kw_done, t - 1)
                w = 128 if t < 2 else NS
                for hp in range(HP):
                    mm = pe.transpose(bank[6 + t % 2][0:w, hp * 128:hp * 128 + 128],
                                      kT[:, hp, t * 128:t * 128 + w], ident)
                mm.then_inc(kt_tr, 1)

            def o_chunk(c):
                u = U_A + QKV_UNITS + c // 2
                pe.wait_ge(lo_done, u + 1)
                if c < 2:
                    pe.wait_ge(pair_free, P_A + QKV_UNITS - 1)
                else:
                    pe.wait_ge(o_kept, c - 1)
                chunk(bank[c % 2][:, 0:T], u % 2, c % 2).then_inc(unit_done if c % 2 else o_even, 1)

            def head_scores(h):
                hp, r = h // 2, slice(64 * (h % 2), 64 * (h % 2) + 64)
                if h == 0:
                    pe.wait_ge(pair_free, P_A + 7)
                    pe.wait_ge(tr_free, 8)
                else:
                    pe.wait_ge(pair_free, P_A + 8)
                    pe.wait_ge(qm_done, 2 * h)
                    pe.wait_ge(p_done, h)
                pe.matmul(bank[4][:, 0:384], sel[:, h, :], neg[:, :], start=True, stop=True)
                pe.matmul(bank[5][:, 0:256], kT[r, hp, 0:128], qT[r, hp, 0:256], start=True, stop=True)
                pe.matmul(bank[5][:, 256:384], kT[r, hp, 128:256], qT[r, hp, 128:256], start=True, stop=True)
                pe.matmul(bank[5][:, 384:448], kT[r, hp, 256:384], qT[r, hp, 256:320],
                          start=True, stop=True).then_inc(head_s, 1)

            def head_outputs(h):
                W = DV + 1
                o = bank[6]
                pe.wait_ge(p_done, h + 1)
                pe.wait_ge(qm_done, 2 * h + 2)
                pe.wait_ge(c0_load[h % 2], 16 * (h // 2 + 1))
                pe.wait_ge(kwm_done, h + 1)
                if h == 0:
                    pe.wait_ge(kw_done, 3)
                    pe.wait_ge(pair_free, P_A + 8)
                else:
                    pe.wait_ge(ot_done, 3 * h)
                    pe.wait_ge(cp_done, h)
                    pe.wait_ge(cn_done, h)
                pe.matmul(o[:, 0:W], pmat[:, 0:128], v_tok[:, 0, h, :], start=True, stop=True)
                pe.matmul(o[:, W:2 * W], pmat[:, 128:256], v_tok[:, 0, h, :], start=True, stop=False)
                pe.matmul(o[:, W:2 * W], pmat[:, 256:384], v_tok[:, 1, h, :], start=False, stop=True)
                pe.matmul(o[:, 2 * W:3 * W], pmat[0:64, 384:512], v_tok[0:64, 2, h, :], start=True, stop=True)
                for a in range(4):
                    pe.matmul(o[0:64, 2 * W:3 * W], qm[:, h % 2, a * NS:a * NS + NS], c0[:, h % 2, a, :],
                              start=False, stop=(a == 3), skip_group_check=True)
                for t in range(2):
                    pe.matmul(bank[2][0:64, 0:DV], kw[:, t, h * 64:h * 64 + 64], v_tok[:, t, h, 0:DV],
                              start=(t == 0), stop=(t == 1))
                for a in range(4):
                    mm = pe.matmul(bank[7][:, a * 128:a * 128 + 128],
                                   kwm[:, h % 2, 2 * a:2 * a + 2, :].rearrange("t b d -> t (b d)"),
                                   v_tok[0:64, 2, h, 0:DV], start=True, stop=True)
                mm.then_inc(head_o, 1)

            def head_turn(h):
                pe.wait_ge(ot_done, 3 * h + 3)
                if h >= 1:
                    pe.wait_ge(z_done, h)
                for t in range(3):
                    w = 128 if t < 2 else NS
                    mm = pe.transpose(bank[3][:, t * 128:t * 128 + w], ot[0:w, t, :], ident[0:w, 0:w])
                mm.then_inc(ot_tr, 1)

            units(U_A, P_A, 0, 1, h_wait=split_at_kt(KT), between=gates)
            pe.wait_ge(x_ready, KT)
            units(U_A, P_A, 1, 4)
            turn_values(P_A + 2, 0)
            units(U_A, P_A, 4, 5)
            turn_values(P_A + 3, 1)
            units(U_A, P_A, 5, 6)
            turn_values(P_A + 4, 2)
            turn_rows()
            units(U_A, P_A, 6, 7)
            turn_values(P_A + 5, 3)
            turn_keys(0)
            turn_keys(1)

            def first_scores():
                turn_keys(2)
                head_scores(0)

            units(U_A, P_A, 7, 8, h_wait=lambda kt: first_scores() if kt == KT // 2 else None)
            o_chunk(0)
            for h in range(H):
                head_outputs(h)
                if h + 1 < H:
                    head_scores(h + 1)
                    o_chunk(h + 1)
                else:
                    pe.wait_ge(p_done, H)
                    for t in range(2):
                        pe.matmul(bank[4][0:1, :], ones[:, 0:1], kw[:, t, :], start=(t == 0), stop=(t == 1))
                    pe.matmul(bank[5][0:8, 0:8], con[0:64, C_LAST:C_LAST + 8], cols[0:64, 2, 64:72],
                              start=True, stop=True)
                if h + 1 < H:
                    head_turn(h)

            def gated_at_kt(kt):
                if kt == 2:
                    head_turn(H - 1)
                    pe.matmul(bank[6][0:8, :], con[0:64, C_BM:C_BM + 8], kw[0:64, 2, :],
                              start=True, stop=True).then_inc(n_mm, 1)
                pe.wait_ge(hl_done, 2 * KT + kt + 1)

            pe.wait_ge(cp_done, H)
            units_to_x(U_OA, P_OA, KT, 0, 4, gated_at_kt)
            pe.wait_ge(n_done, 2)
            ffn(1, split_at_kt(3 * KT), None, lambda: total(2))

            units(U_KV, P_KV, 0, 1, h_wait=split_at_kt(4 * KT), between=lambda: total(3))
            pe.wait_ge(x_ready, 3 * KT)
            for k in range(1, 8):
                units(U_KV, P_KV, k, k + 1)
                if k >= 5:
                    turn_values(P_KV + k - 1, k - 5)

            def last_values():
                turn_values(P_KV + 7, 3)
                pe.wait_ge(tr_free, 16)

            ffn(2, split_at_kt(5 * KT), None, last_values)
            units(U_Q, P_Q, 0, 1, h_wait=split_at_kt(6 * KT), between=lambda: total(4))
            units(U_Q, P_Q, 1, 4)

            def prompt_scores(h):
                if h >= 1:
                    pe.wait_ge(pr_b, h)
                pe.matmul(bank[5][:, 0:128], qa[:, h, 0:128], k_all[:, h, 0:128], start=True, stop=True)
                pe.matmul(bank[5][:, 128:384], qa[:, h, 128:256], k_all[:, h, 0:256],
                          start=True, stop=True).then_inc(pr_s, 1)

            def prompt_turn(h):
                pe.wait_ge(pr_p, h + 1)
                if h >= 1:
                    pe.wait_ge(pr_tc, h)
                for i in range(3):
                    mm = pe.transpose(bank[6][:, i * 128:i * 128 + 128],
                                      pp[:, h % 2, i * 128:i * 128 + 128], ident)
                mm.then_inc(pr_t, 1)

            def prompt_outputs(h):
                pe.wait_ge(pr_tc, h + 1)
                if h >= 1:
                    pe.wait_ge(pr_lo, h)
                pe.matmul(bank[7][:, 0:256], v_tok[:, 0, h, 0:DV], pt[:, h % 2, 0:256], start=True, stop=False)
                pe.matmul(bank[7][:, 128:256], v_tok[:, 1, h, 0:DV], pt[:, h % 2, 256:384],
                          start=False, stop=True).then_inc(pr_o, 1)

            pe.wait_ge(pair_free, P_Q + 3)
            pe.wait_ge(x_ready, 4 * KT)
            prompt_scores(0)
            for h in range(H):
                if h == 6:
                    pe.wait_ge(pair_free, P_Q + 4)
                mm = pe.matmul(bank[4][0:NS, h * NS:h * NS + NS], qa[:, h, TP:T], k_all[:, h, TP:T],
                               start=True, stop=True)
            mm.then_inc(new_s, 1)
            pe.wait_ge(qa_sp, 1)
            def cache_scores(i):
                r, g, j = U_OB + i, i // 4, i % 4
                pe.wait_ge(loaded[r % RAW], loads_after(r))
                keys = raw[:, r % RAW, :].rearrange("p (s g h k) -> p s g h k", s=2, g=NPG, h=4)
                for s in range(2):
                    b = 2 * j + s
                    for k in range(4):
                        h = 4 * g + k
                        mm = pe.matmul(bank[h // 2][0:NS, (h % 2) * PAST:(h % 2) * PAST + PAST],
                                       spread0[:, h, b * NS:b * NS + NS], keys[:, s, :, k, :],
                                       start=(b == 0 and h % 2 == 0), stop=(b == NB - 1),
                                       skip_group_check=True)
                mm.then_inc(kv_used, 1)

            def turn_probs(g):
                pe.wait_ge(sm_e, 4 * g + 4)
                for pg in range(NPG):
                    for k in range(4):
                        mm = pe.transpose(bank[2 * g][:, pg * 256 + k * NS:pg * 256 + k * NS + NS],
                                          ss[:, 4 * g + k, pg * PAGE:pg * PAGE + PAGE], ident[0:NS, 0:NS])
                mm.then_inc(sm_t, 1)
                for k in range(4):
                    mm = pe.transpose(bank[2 * g + 1][0:NS, k * NS:k * NS + NS],
                                      ss[:, 4 * g + k, PAST:PAST + NS], ident[0:NS, 0:NS])
                mm.then_inc(sm_t, 1)

            def cache_outputs(i):
                r, g, j = U_OB + NB + i, i // 4, i % 4
                out = bank[2 * g + 1]
                if j == 0:
                    pe.wait_ge(sm_tn, g + 1)
                    for k in range(4):
                        pe.matmul(out[0:NS, k * 128:k * 128 + 128], pn[:, 4 * g + k, :],
                                  v_tok[0:NS, 2, 4 * g + k, 0:DV], start=(k == 0), stop=False,
                                  skip_group_check=True)
                    pe.wait_ge(sm_tc, 2 * g + 2)
                pe.wait_ge(loaded[r % RAW], loads_after(r))
                for s in range(2):
                    b = 2 * j + s
                    for pg, spread in enumerate((spread0, spread1)):
                        for k in range(4):
                            v = (s * NPG + pg) * 512 + k * 128
                            mm = pe.matmul(out[0:NS, k * 128:k * 128 + 128],
                                           spread[:, 4 * g + k, b * NS:b * NS + NS],
                                           raw[:, r % RAW, v:v + 128],
                                           start=False, stop=(b == NB - 1 and pg == 1), skip_group_check=True)
                mm.then_inc(kv_used, 1)

            def turn_outputs(g):
                pe.wait_ge(sm_oc, 4 * g + 4)
                for k in range(4):
                    h = 4 * g + k
                    mm = pe.transpose(bank[2 * g][:, k * NS:k * NS + NS], o_rows[:, h * 128:h * 128 + 128],
                                      ident[0:NS, 0:NS])
                mm.then_inc(sm_ot, 1)

            for i in range(NB):
                cache_scores(i)
                if i == 6:
                    turn_probs(0)
                if i >= 1:
                    prompt_turn(i - 1)
                    prompt_scores(i)
                    prompt_outputs(i - 1)
            cache_outputs(0)
            prompt_turn(H - 1)
            cache_outputs(1)
            prompt_outputs(H - 1)
            cache_outputs(2)
            turn_probs(1)
            cache_outputs(3)
            cache_outputs(4)
            cache_outputs(5)
            turn_outputs(0)
            cache_outputs(6)
            cache_outputs(7)

            def attended_at_kt(kt):
                if kt == 2:
                    turn_outputs(1)
                pe.wait_ge(sm_lo, kt // 4 + 1)

            pe.wait_ge(pr_lo, H)
            units_to_x(U_OB, P_OB, 4 * KT, 0, 4, attended_at_kt)
            ffn(3, split_at_kt(7 * KT), None, lambda: total(5))
            total(6)

        @block.scalar
        def _(sc):
            chain = Chain(sc, s_act)

            def split(n, n_at, r_val):
                for part in range(2):
                    split_half(n, n_at, r_val, part)

            def split_half(n, n_at, r_val, part):
                w = width(n_at) // 2
                if part == 0:
                    sc.wait_ge(loaded[raw_of(n_at) % RAW], r_val)
                    if n_at >= 2:
                        sc.wait_ge(unit_done, n - 1)
                sc.activation(w_hi[:, n_at % 2, part * w:part * w + w],
                              raw[:, raw_of(n_at) % RAW, part * w:part * w + w], ACT.Copy).then_inc(hi_done, 1)

            def split_at(n):
                if n < U_END:
                    split(n, n, loads_after(raw_of(n)))

            def update(j, m, norm, xr):
                sc.wait_ge(*xr)
                if norm is not None:
                    h_split(m, norm)
                square(j, m)

            def square(j, m):
                c = KT * j + m
                if c >= 2:
                    sc.wait_ge(sum_done, c - 1)
                sc.activation(sq[:, m % 2, :], x[:, m, :], ACT.Square).then_inc(sq_done, 1)

            def h_split(m, norm):
                sc.activation(h_hi[:, m, :], x[:, m, :], ACT.Copy,
                              scale=par[:, P_G + KT * norm + m:P_G + KT * norm + m + 1]).then_inc(hh_done, 1)

            def root_of(j):
                sc.wait_ge(ssq_done, j + 1)
                if j >= 1:
                    sc.wait_ge(rms_done, j)
                sc.activation(root[:, :], bank[6][:, 0:T], ACT.Sqrt, bias=epsc[:, 0:1], scale=1.0 / D
                              ).then_inc(root_done, 1)

            def hidden(f, k, k_at):
                c = k + FK * f
                sc.wait_ge(gate_ready, c + 1)
                sc.activation(act[:, k_at % 2, :], gate[:, k_at % 2, :], ACT.Silu).then_inc(silu_ready, 1)
                sc.wait_ge(hid_ready, c + 1)
                dst = f_hi[:, k, :] if isinstance(k, int) else \
                    f_hi[:, bass.ds(k, 1), :].rearrange("p a t -> p (a t)")
                sc.activation(dst, up[:, k_at % 2, :], ACT.Copy).then_inc(hid_hi, 1)

            def ffn(f, j_out, norm, post, xbase):
                u = U_FFN[f]
                post()
                with sc.Fori(0, (FK - 2) // 4) as i:
                    for j in range(1, 5):
                        n = u + j + 1
                        split(i * 4 + n, n, i * 16 + loads_after(raw_of(n)))
                        hidden(f, i * 4 + (j - 1), j - 1)
                split_at(u + FK)
                hidden(f, FK - 2, FK - 2)
                split_at(u + FK + 1)
                hidden(f, FK - 1, FK - 1)
                split_at(u + FK + 2)
                for m in range(1, KT):
                    split_at(u + FK + 2 * m + 1)
                    update(j_out, m - 1, norm, (x_ready, xbase + m))
                    split_at(u + FK + 2 * m + 2)

            split_at(0)
            sc.wait_ge(s_par, 16)
            for m in range(KT):
                update(0, m, N_A0, (s_x[m], 16))
            sc.wait_ge(s_set, 4)

            def first_post():
                split_at(1)
                root_of(0)

            ffn(0, 1, N_A1, first_post, 0)

            def copy_values(count):
                for c in range(2):
                    g = count * 2 + c
                    h = g % H
                    b = bank[4 + g % 2]
                    sc.wait_ge(tr_done, g + 1)
                    sc.activation(v_tok[:, 0:2, h, 0:DV], b[:, 0:256].rearrange("p (t d) -> p t d", t=2), ACT.Copy)
                    sc.activation(v_tok[0:NS, 2, h, 0:DV], b[0:NS, 256:384], ACT.Copy).then_inc(tr_free, 1)

            def tanh(c):
                sc.wait_ge(o_kept, c + 1)
                sc.activation(og[:, c, :], og[:, c, :], ACT.Tanh, scale=0.5).then_inc(tanh_done, 1)

            split_at(U_A + 1)
            update(1, KT - 1, N_A1, (x_ready, KT))
            root_of(1)
            split_at(U_A + 2)
            sc.wait_ge(abs_done, 1)
            chain.link(sc.activation(fa[:, :], fa[:, :], ACT.Exp, scale=-1.0))
            sc.activation(fa[:, :], fa[:, :], ACT.Ln, bias=1.0).then_inc(ln_done, 1)
            split_at(U_A + 3)
            split_at(U_A + 4)
            sc.wait_ge(zero_done, 4)
            sc.wait_ge(dm_done, 1)
            sc.activation(rows[64:72, :], fa[:, :], ACT.Exp).then_inc(rows_b, 1)
            sc.activation(neg[:, T:384], fa[:, TP:T], ACT.Exp).then_inc(rows_b, 1)
            sc.wait_ge(mt_done, 1)
            sc.activation(rows[96:104, :], mt[:, :], ACT.Exp, scale=-1.0).then_inc(rows_b, 1)
            sc.wait_ge(aw_done, 2)
            sc.activation(rows[32:40, :], g40[0:8, :], ACT.Exp).then_inc(rows_b, 1)
            split_at(U_A + 5)
            copy_values(0)
            split_at(U_A + 6)
            copy_values(1)
            split_at(U_A + 7)
            copy_values(2)
            sc.wait_ge(rows_t, 1)
            sc.activation(cols[:, 0:2, :], bank[6][:, 0:256].rearrange("p (t r) -> p t r", t=2), ACT.Copy
                          ).then_inc(cols_done, 1)
            sc.activation(cols[0:NS, 2, :], bank[6][0:NS, 256:384], ACT.Copy).then_inc(cols_done, 1)
            sc.wait_ge(acb_mm, 1)
            sc.activation(acb[:, :, :], bank[7][:, 0:32].rearrange("p (a h) -> p a h", a=4), ACT.Copy
                          ).then_inc(cols_done, 1)
            split_at(U_A + 8)
            copy_values(3)

            def decay(h):
                sc.wait_ge(d_done, h + 1)
                sc.activation(dmat[:, :], dmat[:, :], ACT.Exp).then_inc(w_done, 1)

            def head_squares(h):
                sc.wait_ge(head_o, h + 1)
                if h >= 1:
                    sc.wait_ge(cp_out_s, 16 * h)
                sc.activation(cpn[:, :], bank[2][0:DK, 0:DV], ACT.Copy).then_inc(cp_done, 1)
                sc.wait_ge(den_done, h + 1)
                for t in range(3):
                    sc.activation(junk[:, t, :], bank[6][:, t * (DV + 1):t * (DV + 1) + DV], ACT.Square,
                                  accum_out=ssqh[:, t:t + 1]).then_inc(ssq_h, 1)

            def head_scale(h):
                sc.wait_ge(s_pow, h + 1)
                if h >= 1:
                    sc.wait_ge(ot_tr, h)
                for t in range(3):
                    sc.activation(ot[:, t, :], bank[6][:, t * (DV + 1):t * (DV + 1) + DV], ACT.Copy,
                                  scale=scl[:, t:t + 1]).then_inc(ot_done, 1)

            def z_split(h):
                sc.wait_ge(z_done, h + 1)
                sc.activation(h_hi[:, h, :], og[:, h, :], ACT.Copy).then_inc(hh_done, 1)

            decay(0)
            split_at(U_A + 9)
            tanh(0)
            for h in range(H):
                head_squares(h)
                if h + 1 < H:
                    head_scale(h)
                    decay(h + 1)
                else:
                    sc.wait_ge(unit_done, U_OA)
                    z_split(0)
                    z_split(1)
                    head_scale(h)
                    for g in range(2, H):
                        z_split(g)
                for k, part in HALVES.get(h, ()):
                    split_half(U_A + k, U_A + k, loads_after(U_A + k), part)
                if h + 1 < H:
                    tanh(h + 1)
            split_at(U_OA + 2)
            for k in range(3):
                for c in range(2):
                    update(2, 2 * k + c, None, (x_ready, KT + 2 * k + c + 1))
                if k < 2:
                    split_at(U_OA + 3 + k)

            def resplit(norm, n, x_last):
                sc.wait_ge(unit_done, n + 1)
                for m in range(KT):
                    if m == KT - 2:
                        sc.wait_ge(x_ready, x_last)
                    h_split(m, norm)

            def after_oa():
                resplit(N_A2, U_OA + 3, 2 * KT)
                square(2, 6)
                square(2, 7)
                split_at(U_FFN[1] + 1)
                root_of(2)
                sc.wait_ge(s_out, 16 * 3)
                sc.wait_ge(cn_out, 16 * H)
                sc.wait_ge(cp_out_s, 16 * H)

            ffn(1, 3, N_KV, after_oa, 2 * KT)

            split_at(U_KV + 1)
            update(3, KT - 1, N_KV, (x_ready, 3 * KT))
            root_of(3)
            for k in range(1, 8):
                split_at(U_KV + k + 1)
                if k >= 6:
                    copy_values(k - 2)

            def after_kv():
                resplit(N_B0, U_KV + 7, 3 * KT)
                split_at(U_FFN[2] + 1)
                copy_values(6)
                copy_values(7)

            ffn(2, 4, N_B1, after_kv, 3 * KT)

            split_at(U_Q + 1)
            update(4, KT - 1, N_B1, (x_ready, 4 * KT))
            root_of(4)
            split_at(U_Q + 2)
            split_at(U_Q + 3)

            def prompt_exp(h):
                sc.wait_ge(pr_m, 2 * h + 2)
                if h >= 2:
                    sc.wait_ge(pr_p, h - 1)
                for c, i in ((slice(0, 128), 0), (slice(128, 384), 1)):
                    sc.activation(pp[:, h % 2, c], pp[:, h % 2, c], ACT.Exp, bias=st[:, h % 2, i:i + 1],
                                  accum_out=st[:, h % 2, 2 + i:3 + i]).then_inc(pr_e, 1)

            def prompt_copy(h):
                sc.wait_ge(pr_t, h + 1)
                if h >= 2:
                    sc.wait_ge(pr_o, h - 1)
                sc.activation(pt[:, h % 2, :], bank[6][:, 0:384], ACT.Copy).then_inc(pr_tc, 1)

            def prompt_hi(h):
                sc.wait_ge(pr_o, h + 1)
                sc.activation(h_hi[:, h, 0:TP], bank[7][:, 0:TP], ACT.Copy).then_inc(pr_hi, 1)

            def sample_exp(h):
                sc.wait_ge(sm_m, h + 1)
                sc.activation(ss[:, h, :], ss[:, h, :], ACT.Exp, bias=sst[:, 0, h:h + 1],
                              accum_out=sst[:, 1, h:h + 1]).then_inc(sm_e, 1)

            def new_weights(g):
                sc.wait_ge(sm_t, 2 * g + 2)
                sc.activation(pn[:, 4 * g:4 * g + 4, :],
                              bank[2 * g + 1][0:NS, 0:256].rearrange("p (h t) -> p h t", h=4), ACT.Copy
                              ).then_inc(sm_tn, 1)

            def sample_rows(g):
                sc.wait_ge(kv_used, NB + 4 * g + 4)
                sc.wait_ge(sm_r, g + 1)
                sc.wait_ge(pr_s, H)
                for k in range(4):
                    h = 4 * g + k
                    sc.activation(o_rows[:, h * 128:h * 128 + 128], bank[2 * g + 1][0:NS, k * 128:k * 128 + 128],
                                  ACT.Copy, scale=sst[:, 2, h:h + 1]).then_inc(sm_oc, 1)

            def sample_hi(g):
                sc.wait_ge(sm_ot, g + 1)
                sc.activation(h_hi[:, 4 * g:4 * g + 4, TP:T],
                              bank[2 * g][:, 0:256].rearrange("p (h t) -> p h t", h=4), ACT.Copy
                              ).then_inc(sm_hi, 1)

            for i in range(NB):
                if i == 6:
                    new_weights(0)
                if i >= 1:
                    prompt_copy(i - 1)
                prompt_exp(i)
                if i in (4, 5):
                    sample_exp(2 * i - 8)
                    sample_exp(2 * i - 7)
                if i >= 1:
                    prompt_hi(i - 1)
            for h in range(4, H):
                sample_exp(h)
            prompt_copy(H - 1)
            prompt_hi(H - 1)
            new_weights(1)
            sample_rows(0)
            split_at(U_OB)
            sample_hi(0)
            split_at(U_OB + 1)
            sample_rows(1)
            sample_hi(1)
            for k in range(3):
                split_at(U_OB + 2 + k)
                for c in range(2):
                    update(5, 2 * k + c, None, (x_ready, 4 * KT + 2 * k + c + 1))

            def after_ob():
                resplit(N_B2, U_OB + 3, 5 * KT)
                square(5, 6)
                square(5, 7)
                split_at(U_FFN[3] + 1)
                root_of(5)

            ffn(3, 6, None, after_ob, 5 * KT)
            update(6, KT - 1, None, (x_ready, 6 * KT))
            root_of(6)

        @block.vector
        def _(ve):
            chain = Chain(ve, s_dve)

            def split(n, n_at):
                split_half(n, n_at, 0)
                split_half(n, n_at, 1)

            def split_half(n, n_at, part):
                w = width(n_at) // 2
                c = slice(part * w, part * w + w)
                ve.wait_ge(hi_done, n * 2 + (part + 1))
                ins = ve.tensor_tensor(w_lo[:, n_at % 2, c], raw[:, raw_of(n_at) % RAW, c],
                                       w_hi[:, n_at % 2, c].bitcast(f32), ALU.subtract)
                if part:
                    ins.then_inc(lo_done, 1)

            def split_at(n):
                if n < U_END:
                    split(n, n)

            def h_lo_of(m, norm, count):
                ve.wait_ge(hh_done, count)
                ve.scalar_tensor_tensor(out=h_lo[:, m, :], in0=x[:, m, :],
                                        scalar=par[:, P_G + KT * norm + m:P_G + KT * norm + m + 1],
                                        in1=h_hi[:, m, :].bitcast(f32), op0=ALU.mult, op1=ALU.subtract
                                        ).then_inc(hl_done, 1)

            def rms_of(j):
                ve.wait_ge(root_done, j + 1)
                ve.reciprocal(rms[:, :], root[:, :]).then_inc(rms_done, 1)
                ve.wait_ge(rms_done, j + 1)

            def scaled(f, k, k_at, p):
                b = 2 * ((P_FFN[f] + k_at) % 2)
                ve.wait_ge(unit_done, k + (U_FFN[f] + 1))
                ve.tensor_tensor(gate[:, k_at % 2, :], bank[b][:, 0:T], rms[:, :], ALU.mult).then_inc(gate_ready, 1)
                ve.tensor_tensor(up[:, k_at % 2, :], bank[b + 1][:, 0:T], rms[:, :], ALU.mult).then_inc(pair_free, 1)

            def hidden(f, k, k_at):
                c = k + FK * f
                ve.wait_ge(pair_free, k + (P_FFN[f] + 1))
                ve.wait_ge(silu_ready, c + 1)
                ve.tensor_tensor(up[:, k_at % 2, :], up[:, k_at % 2, :], act[:, k_at % 2, :], ALU.mult
                                 ).then_inc(hid_ready, 1)
                ve.wait_ge(hid_hi, c + 1)
                if isinstance(k, int):
                    hi, lo = f_hi[:, k, :], f_lo[:, k, :]
                else:
                    hi, lo = (t[:, bass.ds(k, 1), :].rearrange("p a t -> p (a t)") for t in (f_hi, f_lo))
                ve.tensor_tensor(lo, up[:, k_at % 2, :], hi.bitcast(f32), ALU.subtract).then_inc(hid_lo, 1)

            def add_out(f, m):
                ve.wait_ge(unit_done, U_FFN[f] + FK + 2 * m + 2)
                ve.scalar_tensor_tensor(out=x[:, m, :], in0=bank[4 + m % 2][:, 0:T], scalar=0.5,
                                        in1=x[:, m, :], op0=ALU.mult, op1=ALU.add).then_inc(x_ready, 1)

            def add_pair(u, p, k):
                ve.wait_ge(unit_done, u + k + 1)
                b = 2 * ((p + k) % 2)
                for c in range(2):
                    ve.tensor_tensor(x[:, 2 * k + c, :], bank[b + c][:, 0:T], x[:, 2 * k + c, :], ALU.add
                                     ).then_inc(x_ready, 1)

            def ffn(f, norm, hbase, post):
                u, p = U_FFN[f], P_FFN[f]
                post()
                with ve.Fori(0, (FK - 2) // 4) as i:
                    for j in range(1, 5):
                        k, k_at = i * 4 + (j - 1), j - 1
                        scaled(f, k, k_at, p)
                        split(i * 4 + (u + j + 1), u + j + 1)
                        hidden(f, k, k_at)
                for k in (FK - 2, FK - 1):
                    scaled(f, k, k, p)
                    split_at(u + k + 2)
                    hidden(f, k, k)
                split_at(u + FK + 2)
                for m in range(1, KT):
                    add_out(f, m - 1)
                    split_at(u + FK + 2 * m + 1)
                    if norm is not None:
                        h_lo_of(m - 1, norm, hbase + m)
                    split_at(u + FK + 2 * m + 2)

            ve.wait_ge(s_par, 16)
            split_at(0)
            for m in range(KT):
                ve.wait_ge(s_x[m], 16)
                h_lo_of(m, N_A0, m + 1)

            def first_post():
                split_at(1)
                rms_of(0)
                ve.wait_ge(s_con, 48)
                for m in range(KT):
                    ve.tensor_scalar(wg[:, m, :], wg[:, m, :],
                                     par[:, P_G + KT * N_A1 + m:P_G + KT * N_A1 + m + 1], None, ALU.mult
                                     ).then_inc(wgg_done, 1)

            ffn(0, N_A1, KT, first_post)

            def project(k):
                b = 2 * ((P_A + k) % 2)
                ve.wait_ge(unit_done, U_A + k + 1)
                for c in range(2):
                    src = bank[b + c][:, 0:T]
                    if k < 2:
                        ins = ve.scalar_tensor_tensor(out=kT[:, 2 * k + c, 0:T], in0=src,
                                                      scalar=DK ** -0.5, in1=rms[:, :],
                                                      op0=ALU.mult, op1=ALU.mult)
                    elif k < 6:
                        if k >= 4 and c == 0:
                            ve.wait_ge(tr_done, 2 * (k - 3))
                        ins = ve.tensor_tensor(v_st[:, k % 2, c, :], src, rms[:, :], ALU.mult)
                    else:
                        ins = ve.tensor_tensor(qT[:, 2 * (k - 6) + c, :], src, rms[:, :], ALU.mult)
                ins.then_inc(pair_free, 1)

            def keep_gate(c):
                if c % 2:
                    ve.wait_ge(unit_done, U_A + QKV_UNITS + c // 2 + 1)
                else:
                    ve.wait_ge(o_even, c // 2 + 1)
                ve.tensor_tensor(og[:, c, :], bank[c % 2][:, 0:T], rms[:, :], ALU.mult).then_inc(o_kept, 1)

            def gate_half(c):
                ve.wait_ge(tanh_done, c + 1)
                ve.tensor_scalar(og[:, c, :], og[:, c, :], 0.5, 0.5, ALU.mult, ALU.add).then_inc(og_done, 1)

            add_out(0, KT - 1)
            split_at(U_A + 1)
            h_lo_of(KT - 1, N_A1, 2 * KT)
            rms_of(1)
            project(0)
            ve.wait_ge(gates_mm, 1)
            chain.link(ve.tensor_tensor(g40[:, :], bank[7][0:40, 0:T], rms[0:40, :], ALU.mult))
            ve.tensor_scalar(tmp[:, :], g40[0:8, :], par[0:8, P_BI:P_BI + 1], None, ALU.add)
            chain.link(ve.tensor_scalar(fz[:, :], g40[32:40, :], par[32:40, P_BF:P_BF + 1], None, ALU.add))
            ve.scalar_tensor_tensor(out=fa[:, :], in0=fz[:, :], scalar=-1.0, in1=fz[:, :],
                                    op0=ALU.mult, op1=ALU.max).then_inc(abs_done, 1)
            split_at(U_A + 2)
            project(1)
            split_at(U_A + 3)
            ve.wait_ge(ln_done, 1)
            chain.link(ve.scalar_tensor_tensor(out=fz[:, :], in0=fz[:, :], scalar=0.0, in1=fa[:, :],
                                               op0=ALU.min, op1=ALU.subtract))
            chain.link(ve.tensor_tensor_scan(cb[:, :], row[:, R_MUL:R_MUL + T], fz[:, :], 0.0,
                                             ALU.mult, ALU.add))
            chain.link(ve.tensor_tensor(tmp[:, :], tmp[:, :], cb[:, :], ALU.subtract))
            chain.link(ve.tensor_tensor_scan(cm[:, :], row[:, R_NEG:R_NEG + T], tmp[:, :], 0.0,
                                             ALU.add, ALU.max))
            chain.link(ve.tensor_tensor(cm[:, :], cm[:, :], row[:, R_M0:R_M0 + T], ALU.max))
            project(2)
            split_at(U_A + 4)
            ve.tensor_scalar(neg[:, 0:T], cm[:, :], -1.0, None, ALU.mult)
            ve.tensor_tensor(fa[:, :], row[:, R_M0:R_M0 + T], cm[:, :], ALU.subtract).then_inc(dm_done, 1)
            ve.tensor_tensor(mt[:, :], cb[:, :], cm[:, :], ALU.add).then_inc(mt_done, 1)
            seqs = "k (b t) -> k b t"
            ve.tensor_scalar(g40[0:8, 0:TP], tmp[:, 0:TP], cm[:, TP - 1:TP], None, ALU.subtract
                             ).then_inc(aw_done, 1)
            ve.tensor_tensor(g40[0:8, TP:T].rearrange(seqs, b=NB), tmp[:, TP:T].rearrange(seqs, b=NB),
                             cm[:, TP:T].rearrange(seqs, b=NB)[:, :, TS - 1:TS].to_broadcast([8, NB, TS]),
                             ALU.subtract).then_inc(aw_done, 1)
            ve.wait_ge(zero_done, 4)
            ve.tensor_copy(rows[0:8, :], tmp[:, :]).then_inc(rows_a, 1)
            ve.wait_ge(mt_done, 1)
            ve.tensor_copy(mo[:, 0:1], mt[:, TP - 1:TP]).then_inc(mo_done, 1)
            ve.tensor_copy(mo[:, 1:1 + NB].unsqueeze(2), mt[:, TP:T].rearrange(seqs, b=NB)[:, :, TS - 1:TS]
                           ).then_inc(mo_done, 1)
            project(3)
            split_at(U_A + 5)
            ve.wait_ge(rows_b, 2)
            for half in range(2):
                last = neg[:, T:384].rearrange("k (a s t) -> k a s t", a=4, s=2)[:, :, half, TS - 1:TS]
                ve.tensor_tensor(ac_rhs[:, half, :, :], last.to_broadcast([8, 4, H]),
                                 row[:, R_DEL:R_DEL + 8].unsqueeze(1).to_broadcast([8, 4, H]), ALU.mult
                                 ).then_inc(ac_done, 1)
            project(4)
            split_at(U_A + 6)
            project(5)
            split_at(U_A + 7)
            project(6)

            def weigh_keys(t):
                w = 128 if t < 2 else NS
                ve.wait_ge(kt_tr, t + 1)
                ve.tensor_tensor(kw[0:w, t, :].rearrange("p (h d) -> p h d", h=H),
                                 bank[6 + t % 2][0:w, :].rearrange("p (h d) -> p h d", h=H),
                                 cols[0:w, t, 32:40].unsqueeze(2).to_broadcast([w, H, DK]), ALU.mult
                                 ).then_inc(kw_done, 1)

            ve.wait_ge(cols_done, 2)
            weigh_keys(0)
            weigh_keys(1)
            split_at(U_A + 8)
            weigh_keys(2)

            def decay(h):
                hp, r = h // 2, slice(64 * (h % 2), 64 * (h % 2) + 64)
                ve.wait_ge(head_s, h + 1)
                for t, (o, i) in enumerate((((0, 256), 0), ((256, 384), 128), ((384, 448), 256))):
                    ins = ve.scalar_tensor_tensor(
                        out=dmat[:, o[0]:o[1]], in0=bank[4][:, i:i + o[1] - o[0]], scalar=cols[:, t, h:h + 1],
                        in1=con[:, C_CAP + o[0]:C_CAP + o[1]], op0=ALU.add, op1=ALU.min)
                ins.then_inc(d_done, 1)
                for half in range(2):
                    ve.tensor_tensor(
                        qm[64 * half:64 * half + 64, h % 2, :].rearrange("p (a x) -> p a x", a=4)[
                            :, :, 8 * half:8 * half + 8],
                        qT[r, hp, TP:T].rearrange("p (a s t) -> p a s t", a=4, s=2)[:, :, half, :],
                        bank[4][r, T:384].rearrange("p (a s t) -> p a s t", a=4, s=2)[:, :, half, :],
                        ALU.mult).then_inc(qm_done, 1)

            def weights(h):
                ve.wait_ge(w_done, h + 1)
                ve.tensor_tensor(pmat[:, 0:448], bank[5][:, 0:448], dmat[:, :], ALU.mult).then_inc(p_done, 1)

            def outputs(h):
                o3 = bank[6][:, 0:3 * (DV + 1)].rearrange("p (t d) -> p t d", t=3)
                ve.wait_ge(head_o, h + 1)
                chain.link(ve.tensor_scalar(den[:, :].unsqueeze(2), o3[:, :, DV:DV + 1], -1.0, None, ALU.mult))
                ve.tensor_tensor(den[:, :].unsqueeze(2), den[:, :].unsqueeze(2),
                                 o3[:, :, DV:DV + 1], ALU.max).then_inc(den_done, 1)
                ve.wait_ge(den_done, h + 1)
                chain.link(ve.tensor_tensor(den[:, :].unsqueeze(2), den[:, :].unsqueeze(2),
                                            cols[:, :, 96 + h:97 + h], ALU.max))
                chain.link(ve.scalar_tensor_tensor(out=den[:, :], in0=den[:, :], scalar=EPS, in1=den[:, :],
                                                   op0=ALU.mult, op1=ALU.mult))
                ve.wait_ge(ssq_h, 3 * h + 3)
                ve.scalar_tensor_tensor(out=var[:, :], in0=ssqh[:, :], scalar=1.0 / DV, in1=den[:, :],
                                        op0=ALU.mult, op1=ALU.add).then_inc(s_in, 1)

            def states(h):
                if h >= 1:
                    ve.wait_ge(cn_out, 16 * h)
                for a in range(4):
                    ins = ve.scalar_tensor_tensor(
                        out=cn[:, a, :], in0=c0[:, h % 2, a, 0:DV], scalar=acb[:, a, h:h + 1],
                        in1=bank[7][:, a * 128:a * 128 + 128], op0=ALU.mult, op1=ALU.add)
                ins.then_inc(cn_done, 1)

            def gated(h):
                ve.wait_ge(ot_tr, h + 1)
                ve.wait_ge(og_done, h + 1)
                ve.scalar_tensor_tensor(out=og[:, h, :], in0=bank[3][:, 0:T],
                                        scalar=par[:, P_HEAD + h:P_HEAD + h + 1], in1=og[:, h, :],
                                        op0=ALU.mult, op1=ALU.mult).then_inc(z_done, 1)

            def z_split(h):
                ve.wait_ge(hh_done, 2 * KT + h + 1)
                ve.tensor_tensor(h_lo[:, h, :], og[:, h, :], h_hi[:, h, :].bitcast(f32), ALU.subtract
                                 ).then_inc(hl_done, 1)

            decay(0)
            weights(0)
            project(7)
            split_at(U_A + 9)
            keep_gate(0)
            gate_half(0)
            for h in range(H):
                outputs(h)
                if h + 1 < H:
                    decay(h + 1)
                    states(h)
                    weights(h + 1)
                    for k, part in HALVES.get(h, ()):
                        split_half(U_A + k, U_A + k, part)
                    keep_gate(h + 1)
                    gated(h)
                    gate_half(h + 1)
                else:
                    z_split(0)
                    z_split(1)
                    states(h)
                    for g in range(2, H - 1):
                        z_split(g)
                    gated(h)
                    z_split(h)
                    for k, part in HALVES.get(h, ()):
                        split_half(U_A + k, U_A + k, part)
            ve.wait_ge(n_mm, 1)
            chain.link(ve.tensor_copy(al[:, :], bank[5][0:8, 0:8]))
            ve.wait_ge(s_n0, 16)
            chain.link(ve.tensor_tensor(n0[:, :, :], n0[:, :, :],
                                        al[:, :].unsqueeze(2).to_broadcast([NB, H, DK]), ALU.mult))
            ve.tensor_tensor(nn[:, :, :], n0[:, :, :], bank[6][0:8, :].rearrange("p (h d) -> p h d", h=H),
                             ALU.add).then_inc(n_done, 1)
            ve.tensor_copy(npp, bank[4][0:1, :]).then_inc(n_done, 1)
            add_pair(U_OA, P_OA, 0)
            split_at(U_OA + 2)
            add_pair(U_OA, P_OA, 1)
            split_at(U_OA + 3)
            add_pair(U_OA, P_OA, 2)
            split_at(U_OA + 4)

            def after_oa():
                for m in range(KT):
                    if m == 2:
                        add_pair(U_OA, P_OA, 3)
                    h_lo_of(m, N_A2, 3 * KT + m + 1)
                split_at(U_FFN[1] + 1)
                rms_of(2)
                ve.wait_ge(s_out, 16 * 3)
                ve.wait_ge(cn_out, 16 * H)
                ve.wait_ge(cp_out_s, 16 * H)

            ffn(1, N_KV, 4 * KT, after_oa)

            def kv_post(k):
                b = 2 * ((P_KV + k) % 2)
                ve.wait_ge(unit_done, U_KV + k + 1)
                if k >= 6:
                    ve.wait_ge(tr_done, 8 + 2 * (k - 5))
                for c in range(2):
                    dst = k_all[:, 2 * k + c, :] if k < 4 else v_st[:, k % 2, c, :]
                    ins = ve.tensor_tensor(dst, bank[b + c][:, 0:T], rms[:, :], ALU.mult)
                ins.then_inc(pair_free, 1)

            add_out(1, KT - 1)
            split_at(U_KV + 1)
            h_lo_of(KT - 1, N_KV, 5 * KT)
            rms_of(3)
            for k in range(1, 8):
                kv_post(k - 1)
                split_at(U_KV + k + 1)

            def after_kv():
                for m in range(KT):
                    if m == KT - 2:
                        kv_post(7)
                    h_lo_of(m, N_B0, 5 * KT + m + 1)
                split_at(U_FFN[2] + 1)

            ffn(2, N_B1, 6 * KT, after_kv)

            def q_post(k):
                b = 2 * ((P_Q + k) % 2)
                ve.wait_ge(unit_done, U_Q + k + 1)
                for c in range(2):
                    ins = ve.scalar_tensor_tensor(out=qa[:, 2 * k + c, :], in0=bank[b + c][:, 0:T],
                                                  scalar=128 ** -0.5, in1=rms[:, :],
                                                  op0=ALU.mult, op1=ALU.mult)
                ins.then_inc(pair_free, 1)

            def own(spread):
                return spread[:, :, :].rearrange("p h (b x) -> p h b x", b=NB)[:, :, :, 0:TS]

            add_out(2, KT - 1)
            split_at(U_Q + 1)
            h_lo_of(KT - 1, N_B1, 7 * KT)
            rms_of(4)
            q_post(0)
            split_at(U_Q + 2)
            q_post(1)
            split_at(U_Q + 3)
            q_post(2)
            q_post(3)
            ve.wait_ge(pair_free, P_Q + 4)
            ve.wait_ge(spread_set, 2)
            ve.tensor_copy(own(spread0), qa[:, :, TP:T].rearrange("p h (b t) -> p h b t", b=NB)
                           ).then_inc(qa_sp, 1)

            def prompt_bias(h):
                ve.wait_ge(pr_s, h + 1)
                if h >= 2:
                    ve.wait_ge(pr_t, h - 1)
                ve.scalar_tensor_tensor(out=pp[:, h % 2, :], in0=con[:, C_ND:C_ND + 384], scalar=SLOPE[h],
                                        in1=bank[5][:, 0:384], op0=ALU.mult, op1=ALU.add).then_inc(pr_b, 1)
                ve.wait_ge(pr_b, h + 1)
                for i, c in enumerate((slice(0, 128), slice(128, 384))):
                    ve.tensor_reduce(st[:, h % 2, i:i + 1], pp[:, h % 2, c], AX.X, ALU.max, negate=True
                                     ).then_inc(pr_m, 1)

            def prompt_probs(h):
                ve.wait_ge(pr_e, 2 * h + 2)
                chain.link(ve.reciprocal(st[:, h % 2, 4:6], st[:, h % 2, 2:4]))
                for i, c in enumerate((slice(0, 128), slice(128, 384))):
                    ins = ve.tensor_scalar(pp[:, h % 2, c], pp[:, h % 2, c], st[:, h % 2, 4 + i:5 + i], None,
                                           ALU.mult)
                ins.then_inc(pr_p, 1)

            def prompt_lo(h):
                ve.wait_ge(pr_hi, h + 1)
                ve.tensor_tensor(h_lo[:, h, 0:TP], bank[7][:, 0:TP], h_hi[:, h, 0:TP].bitcast(f32),
                                 ALU.subtract).then_inc(pr_lo, 1)

            def sample_bias(h):
                ve.wait_ge(new_s, 1)
                ve.wait_ge(kv_used, 4 * (h // 4) + 4)
                ve.scalar_tensor_tensor(out=ss[:, h, 0:PAST], in0=con[0:NS, C_NDS:C_NDS + PAST],
                                        scalar=SLOPE[h],
                                        in1=bank[h // 2][0:NS, (h % 2) * PAST:(h % 2) * PAST + PAST],
                                        op0=ALU.mult, op1=ALU.add)
                chain.link(ve.scalar_tensor_tensor(
                    out=ss[:, h, PAST:PAST + NS], in0=con[0:NS, C_NDS + PAST:C_NDS + PAST + NS],
                    scalar=SLOPE[h], in1=bank[4][0:NS, h * NS:h * NS + NS], op0=ALU.mult, op1=ALU.add))
                ve.tensor_reduce(sst[:, 0, h:h + 1], ss[:, h, :], AX.X, ALU.max, negate=True).then_inc(sm_m, 1)

            def spread_probs(g):
                ve.wait_ge(sm_t, 2 * g + 1)
                for pg, spread in enumerate((spread0, spread1)):
                    ve.tensor_copy(own(spread)[:, 4 * g:4 * g + 4],
                                   bank[2 * g][:, pg * 256:pg * 256 + 256].rearrange(
                                       "p (h b t) -> p h b t", h=4, b=NB)).then_inc(sm_tc, 1)
                ve.wait_ge(sm_e, 4 * g + 4)
                ve.reciprocal(sst[:, 2, 4 * g:4 * g + 4], sst[:, 1, 4 * g:4 * g + 4]).then_inc(sm_r, 1)

            def sample_lo(g):
                ve.wait_ge(sm_hi, g + 1)
                ve.tensor_tensor(h_lo[:, 4 * g:4 * g + 4, TP:T],
                                 bank[2 * g][:, 0:256].rearrange("p (h t) -> p h t", h=4),
                                 h_hi[:, 4 * g:4 * g + 4, TP:T].bitcast(f32), ALU.subtract).then_inc(sm_lo, 1)

            for i in range(NB):
                if i == 6:
                    spread_probs(0)
                prompt_bias(i)
                if i in (4, 5):
                    sample_bias(2 * i - 8)
                    sample_bias(2 * i - 7)
                prompt_probs(i)
                if i >= 1:
                    prompt_lo(i - 1)
            for h in range(4, H):
                sample_bias(h)
            prompt_lo(H - 1)
            spread_probs(1)
            split_at(U_OB)
            sample_lo(0)
            split_at(U_OB + 1)
            sample_lo(1)
            for k in range(3):
                add_pair(U_OB, P_OB, k)
                split_at(U_OB + 2 + k)

            def after_ob():
                for m in range(KT):
                    if m == 2:
                        add_pair(U_OB, P_OB, 3)
                    h_lo_of(m, N_B2, 7 * KT + m + 1)
                split_at(U_FFN[3] + 1)
                rms_of(5)

            ffn(3, None, 0, after_ob)
            add_out(3, KT - 1)
            rms_of(6)
            for m in range(KT):
                ve.scalar_tensor_tensor(out=x[:, m, :], in0=x[:, m, :],
                                        scalar=par[:, P_G + KT * N_FIN + m:P_G + KT * N_FIN + m + 1],
                                        in1=rms[:, :], op0=ALU.mult, op1=ALU.mult).then_inc(y_done, 1)

        @block.gpsimd
        def _(gp):
            def add_squares(j):
                for m in range(KT):
                    c = KT * j + m
                    gp.wait_ge(sq_done, c + 1)
                    if m == 0:
                        if j >= 1:
                            gp.wait_ge(ssq_done, j)
                        gp.tensor_copy(sqsum[:, :], sq[:, m % 2, :]).then_inc(sum_done, 1)
                    else:
                        gp.wait_ge(sum_done, c)
                        gp.tensor_tensor(sqsum[:, :], sqsum[:, :], sq[:, m % 2, :], ALU.add).then_inc(sum_done, 1)

            gp.memset(epsc[:, :], EPS).then_inc(s_set, 1)
            gp.memset(mhalf[:, :], -0.5).then_inc(s_set, 1)
            gp.memset(v_tok[:, :, :, DV:DV + 1], 1.0).then_inc(s_set, 1)
            gp.memset(v_tok[:, 2, :, 0:DV], 0.0).then_inc(s_set, 1)
            gp.wait_ge(s_set, 4)
            add_squares(0)
            add_squares(1)
            gp.wait_ge(unit_done, U_A)
            gp.memset(rows[:, :], 0.0).then_inc(zero_done, 1)
            gp.memset(kT[:, :, T:384], 0.0).then_inc(zero_done, 1)
            gp.memset(cols[:, 2, :], 1.0).then_inc(zero_done, 1)
            gp.memset(pmat[:, 448:512], 0.0)
            gp.memset(qm[:, :, :], 0.0).then_inc(zero_done, 1)
            gp.dma_start(n0[:, :, :].rearrange("b h d -> b (h d)"), n0_in).then_inc(s_n0, 16)
            for h in range(2):
                gp.dma_start(c0[:, h, :, :], c0_in[h]).then_inc(c0_load[h], 16)
            gp.wait_ge(mo_done, 2)
            gp.dma_start(m_out, mo[:, :]).then_inc(s_out, 16)

            def keys_of(h):
                if h >= 2:
                    gp.wait_ge(head_o, h - 1)
                gp.tensor_tensor(kwm[:, h % 2, :, :],
                                 kw[0:NS, 2, h * DK:h * DK + DK].unsqueeze(1).to_broadcast([NS, NB, DK]),
                                 con[0:NS, C_BM:C_BM + NB].unsqueeze(2).to_broadcast([NS, NB, DK]), ALU.mult
                                 ).then_inc(kwm_done, 1)

            gp.wait_ge(kw_done, 3)
            keys_of(0)
            keys_of(1)
            for h in range(H):
                gp.wait_ge(s_in, h + 1)
                gp.tensor_tensor(scl[:, :], var[:, :], mhalf[:, :], ALU.pow).then_inc(s_pow, 1)
                gp.wait_ge(cp_done, h + 1)
                gp.dma_start(cp_out[h], cpn[:, :]).then_inc(cp_out_s, 16)
                gp.wait_ge(cn_done, h + 1)
                gp.dma_start(cs_out[h], cn[:, :, :]).then_inc(cn_out, 16)
                if h + 2 < H:
                    gp.dma_start(c0[:, h % 2, :, :], c0_in[h + 2]).then_inc(c0_load[h % 2], 16)
                    keys_of(h + 2)
            gp.wait_ge(n_done, 2)
            gp.dma_start(ns_out, nn[:, :, :].rearrange("b h d -> b (h d)")).then_inc(s_out, 16)
            gp.dma_start(np_out, npp).then_inc(s_out, 16)
            add_squares(2)
            add_squares(3)
            gp.wait_ge(tr_free, 16)
            gp.dma_start(k_out, k_all[:, :, :]).then_inc(s_out, 16)
            gp.dma_start(v_out, v_tok[:, :, :, 0:DV]).then_inc(s_out, 16)
            add_squares(4)
            gp.wait_ge(unit_done, U_Q)
            gp.memset(spread0[:, :, :], 0.0).then_inc(spread_set, 1)
            gp.memset(spread1[:, :, :], 0.0).then_inc(spread_set, 1)
            add_squares(5)
            add_squares(6)


def _constants():
    import numpy as np
    con = np.zeros((128, C_COLS), np.float32)
    p = np.arange(128)[:, None]
    con[:, C_ID:C_ID + 128] = np.eye(128)
    con[:, C_ONE:C_ONE + 128] = 1.0
    s, t = p, np.arange(256)[None, :]
    con[:, C_CAP:C_CAP + 256] = np.where(s <= t, 0.0, -BIG)
    con[:, C_CAP + 256:C_CAP + 384] = np.where(s <= t[:, :128], 0.0, -BIG)
    ts = np.arange(NS)[None, :]
    con[:, C_CAP + 384:C_CAP + 448] = np.where((p < NS) & (p // TS == ts // TS) & (p <= ts), 0.0, -BIG)
    masked = -1e30
    con[:, C_ND:C_ND + 128] = np.where(t[:, :128] <= p, t[:, :128] - p, masked)
    con[:, C_ND + 128:C_ND + 384] = np.where(t <= 128 + p, t - 128 - p, masked)
    con[:, C_NDS:C_NDS + 256] = t - (PAST + p % TS)
    con[:, C_NDS + 256:C_NDS + 320] = np.where((p // TS == ts // TS) & (ts <= p), ts - p, masked)
    con[:, C_BM:C_BM + 8] = p // TS == np.arange(8)[None, :]
    con[:, C_LAST:C_LAST + 8] = p == np.arange(8)[None, :] * TS + TS - 1
    row = np.zeros((8, R_COLS), np.float32)
    row[:, R_SEL:R_SEL + 1024] = np.repeat(np.eye(8), 128, axis=1)
    row[:, R_HALF:R_HALF + 64] = 1.0
    row[:, R_HALF + 192:R_HALF + 256] = 1.0
    starts = np.zeros(T, bool)
    starts[0] = True
    starts[TP::TS] = True
    row[:, R_MUL:R_MUL + T] = np.where(starts, 0.0, 1.0)
    row[:, R_NEG:R_NEG + T] = np.where(starts, -BIG, 0.0)
    row[:, R_DEL:R_DEL + 8] = np.eye(8)
    return con, row


def _pair_units(w, first, second):
    import numpy as np
    a = w.reshape(KT, 128, -1)
    out = np.empty((len(first), 128, 2, KT, 128), w.dtype)
    for u, (i, j) in enumerate(zip(first, second)):
        out[u, :, 0] = a[:, :, i:i + 128].transpose(1, 0, 2)
        out[u, :, 1] = a[:, :, j:j + 128].transpose(1, 0, 2)
    return out.reshape(len(first), 128, PAIR)


def _plain_units(w):
    n = w.shape[1] // 256
    return _pair_units(w, [256 * u for u in range(n)], [256 * u + 128 for u in range(n)])


def kernel(**inputs):
    import numpy as np
    import concourse.bacc as bacc
    from concourse import mybir as mb
    from concourse.bass_utils import run_bass_kernel_spmd as run

    a = {k: np.asarray(v) for k, v in inputs.items()}
    w_ffn_in = a["w_ffn_in"].reshape(4, D, 2 * FF)
    w_ffn_out = a["w_ffn_out"].reshape(4, FF, D)
    HK, HV = H * DK, H * DV
    w_in_a = a["w_in_a"][0]
    a_first = [*range(HK, 2 * HK + HV, 256), *range(0, HK, 256), *range(2 * HK + HV, 2 * HK + 2 * HV, 256)]
    gate_w = np.zeros((128, KT, 40), np.float32)
    g = w_in_a[:, 2 * HK + 2 * HV:].reshape(KT, 128, 2 * H).transpose(1, 0, 2)
    gate_w[:, :, 0:8], gate_w[:, :, 32:40] = g[:, :, 0:8], g[:, :, 8:16]
    par = np.zeros((128, P_COLS), np.float32)
    gains = [a["g_norm"][0, 0], a["g_norm"][0, 1], a["g_norm"][0, 2], a["g_kv"],
             a["g_norm"][1, 0], a["g_norm"][1, 1], a["g_norm"][1, 2], a["g_final"]]
    for i, v in enumerate(gains):
        par[:, P_G + KT * i:P_G + KT * i + KT] = v.reshape(KT, 128).T
    par[:, P_HEAD:P_HEAD + H] = a["g_head_a"][0].reshape(H, DV).T
    par[0:8, P_BI] = a["b_gate_a"][0, 0:8]
    par[32:40, P_BF] = a["b_gate_a"][0, 8:16]
    con, row = _constants()
    row[:, R_M0 + TP:R_M0 + T] = np.repeat(a["state_m"][0].T, TS, axis=1)
    xs = np.concatenate([a["x_prompt"].reshape(TP, D), a["x_sample"].reshape(NS, D)])
    c0 = np.empty((H, 2, DK, 4, DV + 1), np.float32)
    c0[..., 0:DV] = a["state_c"][0].reshape(4, 2, H, DK, DV).transpose(2, 1, 3, 0, 4)
    c0[..., DV] = a["state_n"][0].reshape(4, 2, H, DK).transpose(2, 1, 3, 0)
    n_pool = a["cache_k"].shape[0]
    arrays = {
        "w_in": np.stack([_pair_units(w, [128 * i for i in range(FK)], [FF + 128 * i for i in range(FK)])
                          for w in w_ffn_in]),
        "w_out": np.ascontiguousarray(w_ffn_out.reshape(4, 2, HALF, 128, KT, 128).transpose(0, 4, 1, 3, 2, 5)
                                      ).reshape(4, 2 * KT, 128, OUTU),
        "w_a": _pair_units(w_in_a, a_first, [c + 128 for c in a_first]),
        "w_oa": _plain_units(a["w_out_a"][0]),
        "w_kv": _plain_units(a["w_kv"]),
        "w_q": _plain_units(a["w_q_b"][0]),
        "w_ob": _plain_units(a["w_out_b"][0]),
        "w_gate": gate_w,
        "x_in": np.ascontiguousarray(xs.reshape(T, KT, 128).transpose(2, 1, 0)),
        "par_in": par, "con_in": con, "row_in": row,
        "c0_in": c0.reshape(H, 128, 4, DV + 1),
        "n0_in": np.ascontiguousarray(a["state_n"][0].reshape(NB, H * DK)),
        "kc_in": np.ascontiguousarray(a["cache_k"].transpose(0, 3, 2, 1)).reshape(n_pool, 128, H * PAGE),
        "vc_in": np.ascontiguousarray(a["cache_v"]).reshape(n_pool, 128, H * 128),
        "pt_in": np.ascontiguousarray(a["page_table"].reshape(1, NB * NPG)),
    }
    outs = {"y_out": (128, KT, T), "k_out": (128, H, T), "v_out": (128, 3, H, DV), "cp_out": (H, DK, DV),
            "cs_out": (H, 128, 4, DV), "np_out": (1, H * DK), "ns_out": (NB, H * DK), "m_out": (8, 1 + NB)}
    nc = bacc.Bacc("TRN2", target_bir_lowering=False, num_devices=1)
    args = {n: nc.dram_tensor(n, v.shape, mb.dt.from_np(v.dtype), kind="ExternalInput").ap()
            for n, v in arrays.items()}
    args |= {n: nc.dram_tensor(n, s, mb.dt.float32, kind="ExternalOutput").ap() for n, s in outs.items()}
    trunk_program(nc, **args)
    r = run(nc, [arrays], core_ids=[0]).results[0]
    y = r["y_out"].transpose(2, 1, 0).reshape(T, D)
    k = r["k_out"].transpose(2, 1, 0)
    v = r["v_out"].transpose(1, 0, 2, 3).reshape(3 * 128, H, DV)
    cs = r["cs_out"].reshape(H, 2, DK, 4, DV).transpose(3, 1, 0, 2, 4).reshape(1, NB, H, DK, DV)
    out = (y[:TP].reshape(1, TP, D), y[TP:].reshape(NB, TS, D),
           r["cp_out"].reshape(1, 1, H, DK, DV), r["np_out"].reshape(1, 1, H, DK),
           r["m_out"][:, 0].reshape(1, 1, H), k[:TP].reshape(1, TP, H, 128), v[:TP].reshape(1, TP, H, 128),
           cs, r["ns_out"].reshape(1, NB, H, DK), r["m_out"][:, 1:].T.reshape(1, NB, H),
           k[TP:].reshape(NB, TS, H, 128), v[TP:T].reshape(NB, TS, H, 128))
    return tuple(np.ascontiguousarray(o) for o in out)
```
